# Optimizing a Trainium2 kernel written in Bass

```python
import jax
import jax.numpy as jnp
from jax import lax
import numpy as np

D_MODEL = 1024
BATCH = 1
SEQ = 1024
DEPTH = 2
DEC_BATCH = 1
DEC_SEQ = 32
PAST_LEN = 512

CHUNK = 64
CONV_W = 4
A_HEADS = 8
A_DK = 128
A_DV = 128
A_QK = A_HEADS * A_DK
A_VW = A_HEADS * A_DV
A_CONV_CH = 2 * A_QK + A_VW
B_HEADS = 16
B_HD = 64
B_W = B_HEADS * B_HD
BAND_CHUNKS = 8
BAND_ROWS = BAND_CHUNKS * CHUNK
MAX_REL = 128
C_HEADS = 8
C_DK = 128
C_DV = 256
C_QK = C_HEADS * C_DK
C_VW = C_HEADS * C_DV
GATE_RANK = 16
GATE_TAU = 16.0
GLA_BLOCK = 16
MEM_LEN = 256
M_HEADS = 4
M_HD = 128
M_W = M_HEADS * M_HD
EPS = 1e-6

L0_SPLITS = (A_CONV_CH, A_HEADS, A_HEADS, A_VW, B_W, B_W, B_W, B_W)
L1_SPLITS = (C_QK, C_QK, C_VW, GATE_RANK, C_VW)
L0_IN = sum(L0_SPLITS)
L1_IN = sum(L1_SPLITS)

kernel_name = 'hybrid_streaming_encoder_step'

def _split(t, sizes):
    return jnp.split(t, [int(s) for s in np.cumsum(sizes)[:-1]], axis=-1)

def rms_norm(x, g):
    xf = x.astype(jnp.float32)
    y = xf * lax.rsqrt(jnp.mean(xf * xf, axis=-1, keepdims=True) + EPS)
    return (y * g.astype(jnp.float32)).astype(x.dtype)

def l2_norm(x):
    xf = x.astype(jnp.float32)
    return xf * lax.rsqrt(jnp.sum(xf * xf, axis=-1, keepdims=True) + EPS)

def causal_conv(u, buf, w):
    L = u.shape[1]
    ext = jnp.concatenate([buf.astype(u.dtype), u], axis=1)
    y = ext[:, 0:L] * w[0]
    for i in range(1, CONV_W):
        y = y + ext[:, i:i + L] * w[i]
    return y, ext[:, ext.shape[1] - (CONV_W - 1):]

def gdn_block(S, q, k, v, g, beta):
    L = q.shape[1]
    S = S.astype(jnp.float32)
    G = jnp.moveaxis(jnp.cumsum(g, axis=1), 1, -1)
    bt = jnp.moveaxis(beta, 1, -1)
    incl = jnp.tril(jnp.ones((L, L), dtype=bool))
    strict = jnp.tril(jnp.ones((L, L), dtype=bool), -1)
    diff = G[..., :, None] - G[..., None, :]
    dec = jnp.where(incl, jnp.exp(jnp.where(incl, diff, 0.0)), 0.0)
    kk = jnp.einsum('bihd,bjhd->bhij', k, k)
    a_mat = jnp.where(strict, bt[..., :, None] * kk * dec, 0.0) + jnp.eye(L, dtype=jnp.float32)
    rhs = jnp.concatenate([jnp.einsum('bjhv,bhj->bhjv', v, bt),
                           jnp.einsum('bjhd,bhj->bhjd', k, bt * jnp.exp(G))], axis=-1)
    sol = lax.linalg.triangular_solve(a_mat, rhs, left_side=True, lower=True)
    u = sol[..., :A_DV] - jnp.einsum('bhjd,bhdv->bhjv', sol[..., A_DV:], S)
    qk = jnp.einsum('bihd,bjhd->bhij', q, k) * dec
    o = (jnp.einsum('bihd,bhdv->bhiv', q, S) * jnp.exp(G)[..., None]
         + jnp.einsum('bhij,bhjv->bhiv', qk, u))
    g_last = G[..., -1]
    S_new = (S * jnp.exp(g_last)[..., None, None]
             + jnp.einsum('bjhd,bhj,bhjv->bhdv', k, jnp.exp(g_last[..., None] - G), u))
    return S_new, jnp.moveaxis(o, 1, 2)

def gla_block(S, q, k, v, lg):
    L = q.shape[1]
    S = S.astype(jnp.float32)
    cb = jnp.cumsum(lg, axis=1)
    incl = jnp.tril(jnp.ones((L, L), dtype=bool))[None, :, :, None, None]
    diff = cb[:, :, None] - cb[:, None, :]
    dec = jnp.where(incl, jnp.exp(jnp.where(incl, diff, 0.0)), 0.0)
    att = jnp.einsum('bihd,bjhd,bijhd->bhij', q, k, dec)
    o = (jnp.einsum('bihd,bhdv->bihv', q * jnp.exp(cb), S)
         + jnp.einsum('bhij,bjhv->bihv', att, v))
    c_last = cb[:, -1]
    S_new = (S * jnp.exp(c_last)[..., None]
             + jnp.einsum('bjhd,bjhv->bhdv', k * jnp.exp(c_last[:, None] - cb), v))
    return S_new, o

def blocked_scan(block_fn, state0, xs, block):
    n_b, n_t = xs[0].shape[:2]
    nb = n_t // block
    xs_b = tuple(jnp.moveaxis(t.reshape((n_b, nb, block) + t.shape[2:]), 1, 0) for t in xs)
    state, out = lax.scan(lambda s, xb: block_fn(s, *xb), state0, xs_b)
    out = jnp.moveaxis(out, 0, 1)
    return state, out.reshape((n_b, n_t) + out.shape[3:])

def _band_bias(rel_table, n_q, n_k, offset):
    d = jnp.arange(n_q)[:, None] + offset - jnp.arange(n_k)[None, :]
    return rel_table[:, jnp.clip(d, -MAX_REL, MAX_REL) + MAX_REL].astype(jnp.float32)

def _softmax_attend(q, k, v, bias, valid):
    s = jnp.einsum('bqhd,bkhd->bhqk', q, k).astype(jnp.float32) * (q.shape[-1] ** -0.5)
    if bias is not None:
        s = s + bias
    if valid is not None:
        s = jnp.where(valid, s, -jnp.inf)
    p = jax.nn.softmax(s, axis=-1).astype(v.dtype)
    return jnp.einsum('bhqk,bkhd->bqhd', p, v)

def band_attn_prompt(q, k, v, rel_table):
    n_b, n_t, n_h, n_d = q.shape
    n_c = n_t // CHUNK
    n_k = BAND_ROWS + CHUNK
    pad = jnp.zeros((n_b, BAND_ROWS, n_h, n_d), k.dtype)
    kp = jnp.concatenate([pad, k], axis=1)
    vp = jnp.concatenate([pad, v], axis=1)
    bias = _band_bias(rel_table, CHUNK, n_k, BAND_ROWS)

    def one_chunk(c):
        start = c * CHUNK
        qc = lax.dynamic_slice_in_dim(q, start, CHUNK, axis=1)
        kc = lax.dynamic_slice_in_dim(kp, start, n_k, axis=1)
        vc = lax.dynamic_slice_in_dim(vp, start, n_k, axis=1)
        valid = (start - BAND_ROWS + jnp.arange(n_k)) >= 0
        return _softmax_attend(qc, kc, vc, bias, valid)

    out = lax.map(one_chunk, jnp.arange(n_c))
    return jnp.moveaxis(out, 0, 1).reshape(n_b, n_t, n_h, n_d)

def band_attn_sample(q, k, v, k_cache, v_cache, rel_table):
    w = k_cache.shape[1]
    kk = jnp.concatenate([k_cache.astype(k.dtype), k], axis=1)
    vv = jnp.concatenate([v_cache.astype(v.dtype), v], axis=1)
    bias = _band_bias(rel_table, q.shape[1], kk.shape[1], w)
    return _softmax_attend(q, kk, vv, bias, None)

def layer0_mixer(h, conv_buf, S0, band_k_cache, band_v_cache, w_in, conv_w, a_log, dt_bias,
                 a_onorm_g, b_q_g, b_k_g, rel_table, w_out, prompt):
    n_b, L, _ = h.shape
    f32 = jnp.float32
    u, a_raw, b_raw, z_a, q_b, k_b, v_b, z_b = _split(h @ w_in, L0_SPLITS)
    u, new_buf = causal_conv(u, conv_buf, conv_w)
    q_a, k_a, v_a = _split(jax.nn.silu(u), (A_QK, A_QK, A_VW))
    q_a = l2_norm(q_a.reshape(n_b, L, A_HEADS, A_DK)) * (A_DK ** -0.5)
    k_a = l2_norm(k_a.reshape(n_b, L, A_HEADS, A_DK))
    v_a = v_a.reshape(n_b, L, A_HEADS, A_DV).astype(f32)
    beta = jax.nn.sigmoid(b_raw.astype(f32))
    g = -jnp.exp(a_log.astype(f32)) * jax.nn.softplus(a_raw.astype(f32) + dt_bias.astype(f32))
    if prompt:
        S_new, o_a = blocked_scan(gdn_block, S0, (q_a, k_a, v_a, g, beta), CHUNK)
    else:
        S_new, o_a = gdn_block(S0, q_a, k_a, v_a, g, beta)
    o_a = rms_norm(o_a, a_onorm_g).reshape(n_b, L, A_VW).astype(h.dtype) * jax.nn.silu(z_a)
    q_b = rms_norm(q_b.reshape(n_b, L, B_HEADS, B_HD), b_q_g)
    k_b = rms_norm(k_b.reshape(n_b, L, B_HEADS, B_HD), b_k_g)
    v_b = v_b.reshape(n_b, L, B_HEADS, B_HD)
    if prompt:
        o_b = band_attn_prompt(q_b, k_b, v_b, rel_table)
        k_rows, v_rows = k_b[:, -BAND_ROWS:], v_b[:, -BAND_ROWS:]
    else:
        o_b = band_attn_sample(q_b, k_b, v_b, band_k_cache, band_v_cache, rel_table)
        k_rows, v_rows = k_b, v_b
    o_b = o_b.reshape(n_b, L, B_W) * jax.nn.silu(z_b)
    y = jnp.concatenate([o_a, o_b], axis=-1) @ w_out
    return y, new_buf, S_new, k_rows, v_rows

def layer1_mixer(h, S0, w_in, w_gate_up, gate_bias, c_onorm_g, w_out, prompt):
    n_b, L, _ = h.shape
    f32 = jnp.float32
    q, k, v, lr, z = _split(h @ w_in, L1_SPLITS)
    q = q.reshape(n_b, L, C_HEADS, C_DK).astype(f32) * (C_DK ** -0.5)
    k = k.reshape(n_b, L, C_HEADS, C_DK).astype(f32)
    v = v.reshape(n_b, L, C_HEADS, C_DV).astype(f32)
    lg = jax.nn.log_sigmoid((lr @ w_gate_up + gate_bias).astype(f32)) / GATE_TAU
    lg = lg.reshape(n_b, L, C_HEADS, C_DK)
    if prompt:
        S_new, o = blocked_scan(gla_block, S0, (q, k, v, lg), GLA_BLOCK)
    else:
        S_new, o = gla_block(S0, q, k, v, lg)
    o = rms_norm(o, c_onorm_g).reshape(n_b, L, C_VW).astype(h.dtype) * jax.nn.silu(z)
    return o @ w_out, S_new

def memory_kv(mem, mem_norm_g, w_mkv, mk_g):
    n_b, n_m, _ = mem.shape
    k, v = _split(rms_norm(mem, mem_norm_g) @ w_mkv, (M_W, M_W))
    k = rms_norm(k.reshape(n_b, n_m, M_HEADS, M_HD), mk_g)
    return k, v.reshape(n_b, n_m, M_HEADS, M_HD)

def memory_attend(h, mk, mv, w_mq, mq_g, w_mo):
    n_b, L, _ = h.shape
    q, z = _split(h @ w_mq, (M_W, M_W))
    q = rms_norm(q.reshape(n_b, L, M_HEADS, M_HD), mq_g)
    o = _softmax_attend(q, mk.astype(q.dtype), mv.astype(q.dtype), None, None)
    return (o.reshape(n_b, L, M_W) * jax.nn.silu(z)) @ w_mo

def setup_inputs(seed: int = 0) -> dict:
    key = jax.random.key(seed)
    keys = iter(jax.random.split(key, 64))
    f32 = jnp.float32

    def nrm(shape, scale):
        return jax.random.normal(next(keys), shape, f32) * scale

    def gain(n):
        return 1.0 + nrm((n,), 0.02)

    def mixer_dt_bias():
        u = jax.random.uniform(next(keys), (A_HEADS,), f32)
        dt = jnp.exp(u * (np.log(0.1) - np.log(0.001)) + np.log(0.001)).astype(f32)
        return dt + jnp.log(-jnp.expm1(-dt))

    band_cache = min(BAND_ROWS, PAST_LEN)
    D = D_MODEL
    return {
        'x_prompt': nrm((BATCH, SEQ, D), 1.0),
        'x_sample': nrm((DEC_BATCH, DEC_SEQ, D), 1.0),
        'mem_prompt': nrm((BATCH, MEM_LEN, D), 1.0),
        'state_l0_gdn_conv': nrm((DEC_BATCH, CONV_W - 1, A_CONV_CH), 1.0),
        'state_l0_gdn': nrm((DEC_BATCH, A_HEADS, A_DK, A_DV), 0.1),
        'cache_l0_band_k': nrm((DEC_BATCH, band_cache, B_HEADS, B_HD), 1.0),
        'cache_l0_band_v': nrm((DEC_BATCH, band_cache, B_HEADS, B_HD), 1.0),
        'cache_l0_mem_k': nrm((DEC_BATCH, MEM_LEN, M_HEADS, M_HD), 1.0),
        'cache_l0_mem_v': nrm((DEC_BATCH, MEM_LEN, M_HEADS, M_HD), 1.0),
        'state_l1_gla': nrm((DEC_BATCH, C_HEADS, C_DK, C_DV), 0.1),
        'cache_l1_mem_k': nrm((DEC_BATCH, MEM_LEN, M_HEADS, M_HD), 1.0),
        'cache_l1_mem_v': nrm((DEC_BATCH, MEM_LEN, M_HEADS, M_HD), 1.0),
        'l0_norm_g': gain(D),
        'l0_w_in': nrm((D, L0_IN), D ** -0.5),
        'l0_conv_w': nrm((CONV_W, A_CONV_CH), CONV_W ** -0.5),
        'l0_a_log': jnp.log(jax.random.uniform(next(keys), (A_HEADS,), f32, 1.0, 16.0)),
        'l0_dt_bias': mixer_dt_bias(),
        'l0_a_onorm_g': gain(A_DV),
        'l0_b_q_g': gain(B_HD),
        'l0_b_k_g': gain(B_HD),
        'l0_b_rel_bias': nrm((B_HEADS, 2 * MAX_REL + 1), 0.2),
        'l0_w_out': nrm((A_VW + B_W, D), (A_VW + B_W) ** -0.5),
        'l0_mnorm_g': gain(D),
        'l0_mem_norm_g': gain(D),
        'l0_w_mkv': nrm((D, 2 * M_W), D ** -0.5),
        'l0_mk_g': gain(M_HD),
        'l0_w_mq': nrm((D, 2 * M_W), D ** -0.5),
        'l0_mq_g': gain(M_HD),
        'l0_w_mo': nrm((M_W, D), M_W ** -0.5),
        'l1_norm_g': gain(D),
        'l1_w_in': nrm((D, L1_IN), D ** -0.5),
        'l1_w_gate_up': nrm((GATE_RANK, C_QK), GATE_RANK ** -0.5),
        'l1_gate_bias': nrm((C_QK,), 0.1),
        'l1_c_onorm_g': gain(C_DV),
        'l1_w_out': nrm((C_VW, D), C_VW ** -0.5),
        'l1_mnorm_g': gain(D),
        'l1_mem_norm_g': gain(D),
        'l1_w_mkv': nrm((D, 2 * M_W), D ** -0.5),
        'l1_mk_g': gain(M_HD),
        'l1_w_mq': nrm((D, 2 * M_W), D ** -0.5),
        'l1_mq_g': gain(M_HD),
        'l1_w_mo': nrm((M_W, D), M_W ** -0.5),
    }

def reference(x_prompt, x_sample, mem_prompt, state_l0_gdn_conv, state_l0_gdn, cache_l0_band_k,
              cache_l0_band_v, cache_l0_mem_k, cache_l0_mem_v, state_l1_gla, cache_l1_mem_k,
              cache_l1_mem_v, l0_norm_g, l0_w_in, l0_conv_w, l0_a_log, l0_dt_bias, l0_a_onorm_g,
              l0_b_q_g, l0_b_k_g, l0_b_rel_bias, l0_w_out, l0_mnorm_g, l0_mem_norm_g, l0_w_mkv,
              l0_mk_g, l0_w_mq, l0_mq_g, l0_w_mo, l1_norm_g, l1_w_in, l1_w_gate_up, l1_gate_bias,
              l1_c_onorm_g, l1_w_out, l1_mnorm_g, l1_mem_norm_g, l1_w_mkv, l1_mk_g, l1_w_mq,
              l1_mq_g, l1_w_mo):
    f32 = jnp.float32
    mix_params = (
        (l0_w_in, l0_conv_w, l0_a_log, l0_dt_bias, l0_a_onorm_g, l0_b_q_g, l0_b_k_g, l0_b_rel_bias, l0_w_out),
        (l1_w_in, l1_w_gate_up, l1_gate_bias, l1_c_onorm_g, l1_w_out),
    )
    norm_g = (l0_norm_g, l1_norm_g)
    mnorm_g = (l0_mnorm_g, l1_mnorm_g)
    mem_in_params = ((l0_mem_norm_g, l0_w_mkv, l0_mk_g), (l1_mem_norm_g, l1_w_mkv, l1_mk_g))
    mem_q_params = ((l0_w_mq, l0_mq_g, l0_w_mo), (l1_w_mq, l1_mq_g, l1_w_mo))
    sample_mem = ((cache_l0_mem_k, cache_l0_mem_v), (cache_l1_mem_k, cache_l1_mem_v))
    sample_rec = ((state_l0_gdn_conv, state_l0_gdn, cache_l0_band_k, cache_l0_band_v), (state_l1_gla,))

    n_p = x_prompt.shape[0]
    yp, ys = x_prompt, x_sample
    prompt_new, sample_new = [], []
    for l in range(DEPTH):
        hp = rms_norm(yp, norm_g[l])
        hs = rms_norm(ys, norm_g[l])
        if l % 2 == 0:
            buf0 = jnp.zeros((n_p, CONV_W - 1, A_CONV_CH), hp.dtype)
            s0 = jnp.zeros((n_p, A_HEADS, A_DK, A_DV), f32)
            mp, *stp = layer0_mixer(hp, buf0, s0, None, None, *mix_params[l], prompt=True)
            ms, *sts = layer0_mixer(hs, *sample_rec[l], *mix_params[l], prompt=False)
        else:
            s0 = jnp.zeros((n_p, C_HEADS, C_DK, C_DV), f32)
            mp, *stp = layer1_mixer(hp, s0, *mix_params[l], prompt=True)
            ms, *sts = layer1_mixer(hs, *sample_rec[l], *mix_params[l], prompt=False)
        yp = yp + mp
        ys = ys + ms
        mk_p, mv_p = memory_kv(mem_prompt, *mem_in_params[l])
        yp = yp + memory_attend(rms_norm(yp, mnorm_g[l]), mk_p, mv_p, *mem_q_params[l])
        ys = ys + memory_attend(rms_norm(ys, mnorm_g[l]), *sample_mem[l], *mem_q_params[l])
        prompt_new += [*stp, mk_p, mv_p]
        sample_new += sts
    p_gdn_conv, p_gdn, p_band_k, p_band_v, p_mem0_k, p_mem0_v, p_gla, p_mem1_k, p_mem1_v = prompt_new
    s_gdn_conv, s_gdn, s_band_k, s_band_v, s_gla = sample_new
    return (yp, ys, p_gdn_conv, p_gdn, p_band_k, p_band_v, p_mem0_k, p_mem0_v, p_gla, p_mem1_k,
            p_mem1_v, s_gdn_conv, s_gdn, s_band_k, s_band_v, s_gla)


_drawn_inputs = setup_inputs


def setup_inputs(seed=0):
    import zlib

    import numpy as np

    out = dict(_drawn_inputs(seed))
    spreads = {}
    factors = {'l0_a_onorm_g': 5.075,
     'l0_b_q_g': 8.0,
     'l0_b_k_g': 2.795,
     'l0_b_rel_bias': 6.571,
     'l0_mnorm_g': 8.0,
     'l0_mem_norm_g': 2.912,
     'l0_mk_g': 3.034,
     'l0_mq_g': 8.0,
     'l1_c_onorm_g': 5.735,
     'l1_mnorm_g': 8.0,
     'l1_mem_norm_g': 2.672,
     'l1_mk_g': 2.826,
     'l1_mq_g': 8.0}
    for name, (base, spread) in spreads.items():
        noise = np.random.default_rng([zlib.crc32(name.encode()), seed]).standard_normal(out[name].shape)
        drawn = base * np.exp(spread * noise) if base else spread * noise
        out[name] = jnp.asarray(drawn.astype(out[name].dtype))
    for name, factor in factors.items():
        out[name] = (out[name] * factor).astype(out[name].dtype)
    return out
```

```python
import math
from contextlib import ExitStack

import concourse.bass as bass
from concourse import mybir

F32 = mybir.dt.float32
ACT = mybir.ActivationFunctionType
ALU = mybir.AluOpType
AX = mybir.AxisListType
ds = bass.ds

D = 1024
KD = D // 128
NP, NS = 1024, 32
NTOK = NP + NS
TILES = 9
PAD = TILES * 128
CHUNK = 64
NCH = NP // CHUNK
CW = (NCH + 1) * CHUNK
BANKS = [(0, 512), (512, 512), (1024, NS)]
JW = NTOK // 3
JOBS = [(0, JW), (JW, JW), (2 * JW, JW)]
EPS = 1e-6
NEG = -1e30


def wait(eng, sem, value):
    if not isinstance(value, int) or value > 0:
        eng.wait_ge(sem, value)


def semaphores(nc, ctx, prefix):
    made = []

    def sem(name):
        made.append(nc.alloc_semaphore(name=prefix + name))
        return made[-1]

    def give_back():
        nc.clear_and_free_semaphores(made)
        nc.all_engine_barrier()

    ctx.callback(give_back)
    return sem


def rows(t):
    return NS if isinstance(t, int) and t == TILES - 1 else 128


def load_ahead(sp, loads):
    for buf, src, loaded in loads:
        sp.dma_start(buf, src).then_inc(loaded, 16)


def over_tiles(eng, first, second, behind=True):
    def both(*a):
        for t, p, n, do in a if behind else (a[1], a[0]):
            do(t, p, n)

    def two(i):
        both((i * 2 + 1, 1, i, first), (i * 2, 0, i, second))
        both((i * 2 + 2, 0, i + 1, first), (i * 2 + 1, 1, i, second))

    first(0, 0, 0)
    two(0)
    with eng.Fori(1, 3) as i:
        two(i)
    both((7, 1, 3, first), (6, 0, 3, second))
    both((8, 0, 4, first), (7, 1, 3, second))
    second(8, 0, 4)


def identity(nc, ctx, name="ident"):
    ident = ctx.enter_context(nc.sbuf_tensor(name, [128, 128], F32))
    cleared = semaphores(nc, ctx, name)("_cleared")
    with nc.Block() as block:
        @block.gpsimd
        def _(pool):
            pool.memset(ident[:, :], 0.0).then_inc(cleared, 1)
            pool.wait_ge(cleared, 1)
            pool.affine_select(out=ident[:, :], in_=ident[:, :], compare_op=ALU.not_equal, fill=1.0,
                               base=0, pattern=[[-1, 128]], channel_multiplier=1)
    return ident


MEM, M_H, M_D = 256, 4, 128


def memory_kv(nc, ident, eps, mem, layers, ahead):
    with ExitStack() as ctx:
        def sb(n, shape):
            return ctx.enter_context(nc.sbuf_tensor("mkv_" + n, shape, F32))

        sem = semaphores(nc, ctx, "mkv_")

        M = sb("M", [128, 2, D])
        mn = sb("mn", [128, 2, D])
        sqr = sb("sqr", [128, D])
        ss = sb("ss", [128, 3, 2])
        W = [sb(f"W{l}", [128, KD, D]) for l in range(2)]
        g = sb("g", [128, 2, KD])
        kg = sb("kg", [128, 2, M_D])
        mT = [sb(f"mT{l}", [128, KD, MEM]) for l in range(2)]
        sk = sb("sk", [128, 2, M_H, M_D])
        ks = sb("ks", [128, 3, 4, M_H])
        Ko = sb("Ko", [128, 4, 512])
        Vo = sb("Vo", [128, 4, 512])
        TP = ctx.enter_context(nc.psum_tensor("mkv_TP", [128, 2, KD, 128], F32))
        KV = ctx.enter_context(nc.psum_tensor("mkv_KV", [128, 2, 1024], F32))
        m_ld, s_ld, w_ld = sem("m_ld"), sem("s_ld"), [sem("w_ld0"), sem("w_ld1")]
        ssq, root, rstd, scaled, turned, mt_ok = sem("ssq"), sem("root"), sem("rstd"), sem("scaled"), sem("turned"), sem("mt_ok")
        kv_done, ksq, ksum, kroot, krs, k_ok, v_ok, st = (sem("kv_done"), sem("ksq"), sem("ksum"), sem("kroot"), sem("krs"),
                                                         sem("k_ok"), sem("v_ok"), sem("st"))

        with nc.Block() as block:
            @block.sync
            def _(sp):
                sp.dma_start(M[:, :, :], mem.rearrange("(m p) d -> p m d", p=128)).then_inc(m_ld, 16)
                for l, (mg, w, key_g, _, _) in enumerate(layers):
                    sp.dma_start(g[:, l, :], mg.rearrange("(k p) -> p k", p=128), allow_slow_non_contiguous=True).then_inc(s_ld, 16)
                    sp.dma_start(kg[:, l, :], key_g.unsqueeze(0).to_broadcast([128, M_D])).then_inc(s_ld, 16)
                for l, (_, w, _, _, _) in enumerate(layers):
                    sp.dma_start(W[l][:, :, :], w.rearrange("(k p) n -> p k n", p=128)).then_inc(w_ld[l], 16)
                load_ahead(sp, ahead)
                for n in range(4):
                    l, m = n // 2, n % 2
                    _, _, _, k_out, v_out = layers[l]
                    sp.wait_ge(v_ok, n + 1)
                    sp.dma_start(v_out[128 * m:128 * m + 128, :], Vo[:, n, :]).then_inc(st, 16)
                    sp.wait_ge(k_ok, 2 * n + 2)
                    sp.dma_start(k_out[128 * m:128 * m + 128, :], Ko[:, n, :]).then_inc(st, 16)
                sp.wait_ge(st, 8 * 16)

            @block.scalar
            def _(act):
                act.wait_ge(m_ld, 16)
                for m in range(2):
                    act.wait_ge(ssq, m) if m else None
                    act.activation(sqr[:, :], M[:, m, :], ACT.Square, accum_out=ss[:, 0, m:m + 1]).then_inc(ssq, 1)
                act.wait_ge(ssq, 2)
                act.activation(ss[:, 1, :], ss[:, 0, :], ACT.Sqrt, scale=1.0 / D, bias=eps[:, 0:1]).then_inc(root, 1)
                act.wait_ge(rstd, 1)
                for m in range(2):
                    act.activation(mn[:, m, :], M[:, m, :], ACT.Copy, scale=ss[:, 2, m:m + 1]).then_inc(scaled, 1)
                for n in range(4):
                    b = n % 2
                    act.wait_ge(kv_done, n + 1)
                    if n >= 2:
                        act.wait_ge(ksum, n - 1)
                    act.activation(sk[:, b, :, :], KV[:, b, 0:512].rearrange("p (h d) -> p h d", h=M_H), ACT.Square).then_inc(ksq, 1)
                    act.activation(Vo[:, n, :], KV[:, b, 512:1024], ACT.Copy).then_inc(v_ok, 1)
                    act.wait_ge(ksum, n + 1)
                    act.activation(ks[:, 1, n, :], ks[:, 0, n, :], ACT.Sqrt, scale=1.0 / M_D, bias=eps[:, 0:1]).then_inc(kroot, 1)

            @block.tensor
            def _(pe):
                for m in range(2):
                    pe.wait_ge(scaled, m + 1)
                    for k in range(KD):
                        mm = pe.transpose(TP[:, m, k, :], mn[:, m, 128 * k:128 * k + 128], ident[:, :])
                    mm.then_inc(turned, 1)
                for n in range(4):
                    l, m = n // 2, n % 2
                    pe.wait_ge(w_ld[l], 16)
                    pe.wait_ge(mt_ok, 2 * l + 2)
                    if n >= 2:
                        pe.wait_ge(k_ok, 2 * (n - 2) + 1)
                        pe.wait_ge(v_ok, n - 1)
                    for c in range(2):
                        for k in range(KD):
                            mm = pe.matmul(KV[:, n % 2, 512 * c:512 * c + 512], mT[l][:, k, 128 * m:128 * m + 128],
                                           W[l][:, k, 512 * c:512 * c + 512], start=k == 0, stop=k == KD - 1)
                    mm.then_inc(kv_done, 1)

            @block.vector
            def _(dve):
                dve.wait_ge(root, 1)
                dve.reciprocal(ss[:, 2, :], ss[:, 1, :]).then_inc(rstd, 1)
                dve.wait_ge(s_ld, 64)
                for l in range(2):
                    for m in range(2):
                        dve.wait_ge(turned, m + 1)
                        dve.tensor_tensor(mT[l][:, :, 128 * m:128 * m + 128], TP[:, m, :, :],
                                          g[:, l, :].unsqueeze(2).broadcast_to([128, KD, 128]), ALU.mult).then_inc(mt_ok, 1)
                for n in range(4):
                    b, l = n % 2, n // 2
                    dve.wait_ge(ksq, n + 1)
                    dve.tensor_reduce(ks[:, 0, n, :], sk[:, b, :, :], AX.X, ALU.add).then_inc(ksum, 1)
                    dve.wait_ge(kroot, n + 1)
                    dve.reciprocal(ks[:, 2, n, :], ks[:, 1, n, :]).then_inc(krs, 1)
                    dve.wait_ge(krs, n + 1)
                    kv = Ko[:, n, :].rearrange("p (h d) -> p h d", h=M_H)
                    dve.wait_ge(v_ok, n + 1)
                    dve.tensor_tensor(kv, KV[:, b, 0:512].rearrange("p (h d) -> p h d", h=M_H),
                                      ks[:, 2, n, :].unsqueeze(2).broadcast_to([128, M_H, M_D]), ALU.mult).then_inc(k_ok, 1)
                    dve.wait_ge(k_ok, 2 * n + 1)
                    dve.tensor_tensor(kv, kv, kg[:, l, :].unsqueeze(1).broadcast_to([128, M_H, M_D]), ALU.mult).then_inc(k_ok, 1)


QUERY_ORDER = [4, 5, 6, 7, 0, 1, 2, 3]


def query_weights(W, w_ld, w_mq):
    w = w_mq.rearrange("(k p) n -> p k n", p=128)
    cols = [128 * QUERY_ORDER[2 * q] for q in range(4)]
    return [(W[:, :, c:c + 256], w[:, :, c:c + 256], w_ld[q]) for q, c in enumerate(cols)]


def memory_attend(nc, name, ident, ones, eps, hT, W, w_ld, mq_g, kv_prompt, kv_sample, o_dram):
    with ExitStack() as ctx:
        def sb(n, shape):
            return ctx.enter_context(nc.sbuf_tensor(f"{name}_{n}", shape, F32))

        sem = semaphores(nc, ctx, name + "_")

        raw = sb("raw", [128, 2, 2, M_H * M_D])
        V = sb("V", [128, 2, 2, M_H * M_D])
        KT = sb("KT", [128, 2, M_H, MEM])
        QR = sb("QR", [128, 2, 512])
        sqr = sb("sqr", [128, 2, 512])
        rs = sb("rs", [128, 2, 512])
        QN = sb("QN", [128, M_H, NTOK])
        ZS = sb("ZS", [128, M_H, NTOK])
        g = sb("g", [128, 1])
        lns = sb("lns", [128, 1])
        Q1 = sb("Q1", [128, 2, M_H, 128])
        nm = sb("nm", [128, 2, M_H])
        rsum = sb("rsum", [128, 2, M_H])
        rinv = sb("rinv", [128, 2, M_H])
        E = sb("E", [128, 2, M_H, MEM])
        ET = sb("ET", [128, 2, 2, M_H, 128])
        OS = sb("OS", [128, 2, M_H, 128])
        pj = ctx.enter_context(nc.psum_tensor(f"{name}_pj", [128, 2, 512], F32))
        psq = ctx.enter_context(nc.psum_tensor(f"{name}_psq", [128, 512], F32))
        g_ld, k_ld, v_ld = sem("g_ld"), sem("k_ld"), sem("v_ld")
        proj, q_raw, q_sq, q_sum, q_ln, q_rs, q_ok, z_ok = (sem("proj"), sem("q_raw"), sem("q_sq"), sem("q_sum"), sem("q_ln"),
                                                           sem("q_rs"), sem("q_ok"), sem("z_ok"))
        ktp, kt_ok, c_ok = sem("ktp"), sem("kt_ok"), sem("c_ok")
        staged, s_done, nm_ok, e_ok, ri_ok, p_ok = sem("staged"), sem("s_done"), sem("nm_ok"), sem("e_ok"), sem("ri_ok"), sem("p_ok")
        et_done, et_ok, o_done, o_ok, st = sem("et_done"), sem("et_ok"), sem("o_done"), sem("o_ok"), [sem("st0"), sem("st1")]
        order = QUERY_ORDER

        with nc.Block() as block:
            @block.sync
            def _(sp):
                sp.dma_start(g[:, :], mq_g.unsqueeze(1)).then_inc(g_ld, 16)
                for r, (k, v) in enumerate((kv_prompt, kv_sample)):
                    sp.dma_start(raw[:, r, :, :], k.rearrange("(m p) d -> p m d", p=128)).then_inc(k_ld, 16)
                    sp.dma_start(V[:, r, :, :], v.rearrange("(m p) d -> p m d", p=128)).then_inc(v_ld, 16)
                sp.wait_ge(v_ld, 32)

            @block.tensor
            def _(pe):
                def sum_squares(n):
                    w = JOBS[n % 3][1]
                    pe.wait_ge(q_sq, n + 1)
                    wait(pe, q_ln, n)
                    pe.matmul(psq[:, 0:w], ones[:, :], sqr[:, n % 2, 0:w], start=True, stop=True).then_inc(q_sum, 1)

                for m in range(24):
                    j, (c0, w) = order[m // 3], JOBS[m % 3]
                    if m % 6 == 0:
                        pe.wait_ge(w_ld[m // 6], 16)
                    if m >= 2:
                        n = m - 2
                        if n < 12:
                            pe.wait_ge(z_ok, n + 1)
                        else:
                            pe.wait_ge(q_sq, n - 11)
                    for k in range(KD):
                        mm = pe.matmul(pj[:, m % 2, 0:w], W[:, k, 128 * j:128 * j + 128], hT[:, k, c0:c0 + w],
                                       start=k == 0, stop=k == KD - 1)
                    mm.then_inc(proj, 1)
                    if m >= 13:
                        sum_squares(m - 13)
                sum_squares(11)
                pe.wait_ge(k_ld, 32)
                for r in range(2):
                    pe.wait_ge(q_sq, 12)
                    pe.wait_ge(z_ok, 12)
                    for h in range(M_H):
                        if h % 2 == 0 and (r or h):
                            pe.wait_ge(kt_ok, 2 * r + h // 2)
                        for m in range(2):
                            mm = pe.transpose(pj[:, h // 2, 256 * (h % 2) + 128 * m:256 * (h % 2) + 128 * m + 128],
                                              raw[:, r, m, 128 * h:128 * h + 128], ident[:, :])
                        if h % 2:
                            mm.then_inc(ktp, 1)

            @block.scalar
            def _(act):
                for m in range(12):
                    j, (c0, w) = order[m // 3], JOBS[m % 3]
                    act.wait_ge(proj, m + 1)
                    act.activation(ZS[:, j - M_H, c0:c0 + w], pj[:, m % 2, 0:w], ACT.Silu).then_inc(z_ok, 1)
                act.preload_act_table_set("natural_log_exp_and_others")
                act.wait_ge(c_ok, 1)

                def rsqrt(n):
                    w = JOBS[n % 3][1]
                    act.wait_ge(q_sum, n + 1)
                    wait(act, q_ok, n - 1)
                    act.activation(rs[:, n % 2, 0:w], psq[:, 0:w], ACT.Ln, scale=1.0 / M_D, bias=eps[:, 0:1]).then_inc(q_ln, 1)
                    act.wait_ge(q_ln, n + 1)
                    act.activation(rs[:, n % 2, 0:w], rs[:, n % 2, 0:w], ACT.Exp, scale=-0.5, bias=lns[:, 0:1]).then_inc(q_rs, 1)

                for n in range(12):
                    w = JOBS[n % 3][1]
                    act.wait_ge(proj, 12 + n + 1)
                    wait(act, q_ok, n - 1)
                    act.activation(QR[:, n % 2, 0:w], pj[:, n % 2, 0:w], ACT.Copy).then_inc(q_raw, 1)
                    wait(act, q_sum, n - 1)
                    act.activation(sqr[:, n % 2, 0:w], pj[:, n % 2, 0:w], ACT.Square).then_inc(q_sq, 1)
                    if n:
                        rsqrt(n - 1)
                rsqrt(11)

            @block.vector
            def _(dve):
                dve.memset(lns[:, :], -0.5 * math.log(M_D)).then_inc(c_ok, 1)
                dve.wait_ge(g_ld, 16)
                for n in range(12):
                    j, (c0, w) = n // 3, JOBS[n % 3]
                    dve.wait_ge(q_raw, n + 1)
                    dve.wait_ge(q_rs, n + 1)
                    dve.scalar_tensor_tensor(QN[:, j, c0:c0 + w], QR[:, n % 2, 0:w], g[:, 0:1], rs[:, n % 2, 0:w],
                                             ALU.mult, ALU.mult).then_inc(q_ok, 1)
                for r in range(2):
                    for h in range(0, M_H, 2):
                        dve.wait_ge(ktp, 2 * r + h // 2 + 1)
                        dve.tensor_copy(KT[:, r, h:h + 2, :], pj[:, h // 2, :].rearrange("p (h n) -> p h n", h=2)).then_inc(kt_ok, 1)

        SC = [ctx.enter_context(nc.psum_tensor(f"{name}_SC{p}", [128, M_H, MEM], F32)) for p in range(1)]
        PT = ctx.enter_context(nc.psum_tensor(f"{name}_PT", [128, 2, M_H, 128], F32))
        PO = pj[:, 0, :].rearrange("p (h n) -> p h n", h=M_H)

        def cols_of(t):
            return slice(NP, NTOK) if rows(t) == NS else ds(t * 128, 128)

        with nc.Block() as block:
            @block.sync
            def _(sp):
                def first(t, p, n):
                    sp.wait_ge(o_ok, t + 1)
                    sp.dma_start(o_dram[0:M_H * M_D, cols_of(t)].rearrange("(h p) t -> p h t", p=128),
                                 OS[:, p, :, 0:rows(t)]).then_inc(st[p], 16)

                over_tiles(sp, first, lambda t, p, n: None)
                sp.wait_ge(st[0], 5 * 16)
                sp.wait_ge(st[1], 4 * 16)

            @block.gpsimd
            def _(pool):
                def first(t, p, n):
                    r = rows(t)
                    if not (isinstance(t, int) and t < 2):
                        pool.wait_ge(s_done, t - 1)
                    pool.tensor_copy(Q1[:, p, :, 0:r], QN[:, :, cols_of(t)]).then_inc(staged, 1)

                over_tiles(pool, first, lambda t, p, n: None)

            @block.tensor
            def _(pe):
                def first(t, p, n):
                    r, q = rows(t), int(rows(t) == NS)
                    pe.wait_ge(staged, t + 1)
                    if not (isinstance(t, int) and t == 0):
                        pe.wait_ge(e_ok, t * M_H)
                    for h in range(M_H):
                        mm = pe.matmul(SC[0][0:r, h, :], Q1[:, p, h, 0:r], KT[:, q, h, :], start=True, stop=True)
                    mm.then_inc(s_done, 1)

                def second(t, p, n):
                    r, q = rows(t), int(rows(t) == NS)
                    pe.wait_ge(p_ok, t + 1)
                    if not (isinstance(t, int) and t == 0):
                        pe.wait_ge(et_ok, t)
                    for m in range(2):
                        for h in range(M_H):
                            mm = pe.transpose(PT[:, m, h, 0:r], E[0:r, p, h, 128 * m:128 * m + 128], ident[0:r, 0:r])
                    mm.then_inc(et_done, 1)
                    pe.wait_ge(et_ok, t + 1)
                    if not (isinstance(t, int) and t == 0):
                        pe.wait_ge(o_ok, t)
                    for h in range(M_H):
                        for m in range(2):
                            mm = pe.matmul(PO[:, h, 0:r], V[:, q, m, 128 * h:128 * h + 128], ET[:, p, m, h, 0:r],
                                           start=m == 0, stop=m == 1)
                    mm.then_inc(o_done, 1)

                over_tiles(pe, first, second)

            @block.scalar
            def _(act):
                act.preload_act_table_set("natural_log_exp_and_others")

                def first(t, p, n):
                    r = rows(t)
                    act.wait_ge(nm_ok, t + 1)
                    if not (isinstance(t, int) and t < 2):
                        act.wait_ge(et_done, t - 1)
                        act.wait_ge(ri_ok, t - 1)
                    for h in range(M_H):
                        act.activation(E[0:r, p, h, :], SC[0][0:r, h, :], ACT.Exp, bias=nm[0:r, p, h:h + 1],
                                       accum_out=rsum[0:r, p, h:h + 1]).then_inc(e_ok, 1)

                def second(t, p, n):
                    r = rows(t)
                    act.wait_ge(et_done, t + 1)
                    if not (isinstance(t, int) and t < 2):
                        act.wait_ge(o_done, n * 2)
                    act.activation(ET[:, p, :, :, 0:r], PT[:, :, :, 0:r], ACT.Copy).then_inc(et_ok, 1)

                over_tiles(act, first, second, behind=False)

            @block.vector
            def _(dve):
                def first(t, p, n):
                    r = rows(t)
                    dve.wait_ge(s_done, t + 1)
                    if not (isinstance(t, int) and t < 2):
                        dve.wait_ge(e_ok, (t - 1) * M_H)
                    dve.tensor_reduce(nm[0:r, p, :], SC[0][0:r, :, :], AX.X, ALU.max, negate=True).then_inc(nm_ok, 1)
                    dve.wait_ge(e_ok, (t + 1) * M_H)
                    dve.reciprocal(rinv[0:r, p, :], rsum[0:r, p, :]).then_inc(ri_ok, 1)
                    dve.wait_ge(ri_ok, t + 1)
                    dve.tensor_tensor(E[0:r, p, :, :], E[0:r, p, :, :], rinv[0:r, p, :].unsqueeze(2).broadcast_to([r, M_H, MEM]),
                                      ALU.mult).then_inc(p_ok, 1)

                def second(t, p, n):
                    r = rows(t)
                    dve.wait_ge(o_done, t + 1)
                    wait(dve, st[p], n * 16)
                    dve.tensor_tensor(OS[:, p, :, 0:r], PO[:, :, 0:r], ZS[:, :, cols_of(t)], ALU.mult).then_inc(o_ok, 1)

                over_tiles(dve, first, second)


def token_rows(pair, t):
    if isinstance(t, int) and t == TILES - 1:
        return pair[1]
    return pair[0][ds(t * 128, 128), :]


PARTS = 4


def out_weights(W, loaded, w_out, kt, q):
    per = kt // PARTS
    return W, w_out.rearrange("(k p) n -> p k n", p=128)[:, per * q:per * q + per, :], loaded


def project_out(nc, name, ident, eps, kt, w_out, parts, o_dram, x_in, x_out, gain, hT, ahead=()):
    with ExitStack() as ctx:
        def sb(n, shape):
            return ctx.enter_context(nc.sbuf_tensor(f"{name}_{n}", shape, F32))

        sem = semaphores(nc, ctx, name + "_")

        per = kt // PARTS
        parts = list(parts)
        given = len(parts)
        while kt and len(parts) < PARTS:
            parts.append((sb(f"W{len(parts)}", [128, per, D]), sem(f"w_ld{len(parts)}")))
        oS = [sb(f"oS{p}", [128, kt, 128]) if kt else None for p in range(2)]
        xS = [sb(f"xS{p}", [128, D]) for p in range(2)]
        xn = [sb(f"xn{p}", [128, D]) for p in range(2)]
        sqr = sb("sqr", [128, D])
        ss = sb("ss", [128, 2, 3])
        g = sb("g", [128, KD])
        Y = [ctx.enter_context(nc.psum_tensor(f"{name}_Y{p}", [128, D], F32)) for p in range(2)]
        TP = [ctx.enter_context(nc.psum_tensor(f"{name}_TP{p}", [128, KD, 128], F32)) for p in range(2)]
        g_ld = sem("g_ld")
        o_ld, x_ld, st = [sem("o_ld0"), sem("o_ld1")], [sem("x_ld0"), sem("x_ld1")], [sem("st0"), sem("st1")]
        y_done, x_new, ssq, root, rstd = sem("y_done"), sem("x_new"), sem("ssq"), sem("root"), sem("rstd")
        scaled, turned, h_out, cleared = sem("scaled"), sem("turned"), sem("h_out"), sem("cleared")

        with nc.Block() as block:
            @block.sync
            def _(sp):
                def load(t, p, n):
                    r = rows(t)
                    if kt:
                        if not (isinstance(t, int) and t < 2):
                            sp.wait_ge(y_done, t - 1)
                        cols = slice(NP, NTOK) if r == NS else ds(t * 128, 128)
                        sp.dma_start(oS[p][:, :, 0:r], o_dram[0:kt * 128, cols].rearrange("(k p) t -> p k t", p=128)).then_inc(o_ld[p], 16)
                    if not (isinstance(t, int) and t < 2):
                        if x_out is not None:
                            sp.wait_ge(st[p], n * 16)
                        if gain is not None:
                            sp.wait_ge(scaled, t - 1)
                    sp.dma_start(xS[p][0:r, :], token_rows(x_in, t)).then_inc(x_ld[p], 16)

                load(0, 0, 0)
                for q in range(given, len(parts)):
                    load_ahead(sp, [out_weights(parts[q][0][:, :, :], parts[q][1], w_out, kt, q)])
                load(1, 1, 0)
                with sp.Fori(0, 3) as i:
                    load(i * 2 + 2, 0, i + 1)
                    load(i * 2 + 3, 1, i + 1)
                load(8, 0, 4)
                load_ahead(sp, ahead)

            @block.tensor
            def _(pe):
                def first(t, p, n):
                    if not kt:
                        return
                    r = rows(t)
                    pe.wait_ge(o_ld[p], n * 16 + 16)
                    if not (isinstance(t, int) and t < 2):
                        pe.wait_ge(x_new, t - 1)
                    for k in range(kt):
                        W, loaded = parts[k // per]
                        if isinstance(t, int) and t == 0 and k % per == 0:
                            pe.wait_ge(loaded, 16)
                        for c in range(0, D, 512):
                            mm = pe.matmul(Y[p][0:r, c:c + 512], oS[p][:, k, 0:r], W[:, k % per, c:c + 512],
                                           start=k == 0, stop=k == kt - 1)
                    mm.then_inc(y_done, 1)

                def second(t, p, n):
                    if gain is None:
                        return
                    r = rows(t)
                    pe.wait_ge(scaled, t + 1)
                    if not (isinstance(t, int) and t < 2):
                        pe.wait_ge(h_out, n * 2)
                    for k in range(KD):
                        mm = pe.transpose(TP[p][:, k, 0:r], xn[p][0:r, 128 * k:128 * k + 128], ident[0:r, 0:r])
                    mm.then_inc(turned, 1)

                over_tiles(pe, first, second)

            @block.scalar
            def _(act):
                if gain is not None:
                    act.dma_start(g[:, :], gain.rearrange("(k p) -> p k", p=128), allow_slow_non_contiguous=True).then_inc(g_ld, 16)

                def first(t, p, n):
                    r = rows(t)
                    if kt:
                        act.wait_ge(x_new, t + 1)
                    else:
                        act.wait_ge(x_ld[p], n * 16 + 16)
                    if x_out is not None:
                        act.dma_start(token_rows(x_out, t), xS[p][0:r, :]).then_inc(st[p], 16)
                    if gain is None:
                        return
                    if not (isinstance(t, int) and t == 0):
                        act.wait_ge(ssq, t)
                    act.activation(sqr[0:r, :], xS[p][0:r, :], ACT.Square, accum_out=ss[0:r, p, 0:1]).then_inc(ssq, 1)
                    act.wait_ge(ssq, t + 1)
                    act.activation(ss[0:r, p, 1:2], ss[0:r, p, 0:1], ACT.Sqrt, scale=1.0 / D, bias=eps[0:r, 0:1]).then_inc(root, 1)

                def second(t, p, n):
                    if gain is None:
                        return
                    r = rows(t)
                    act.wait_ge(rstd, t + 1)
                    if not (isinstance(t, int) and t < 2):
                        act.wait_ge(turned, t - 1)
                    act.activation(xn[p][0:r, :], xS[p][0:r, :], ACT.Copy, scale=ss[0:r, p, 2:3]).then_inc(scaled, 1)

                act.wait_ge(cleared, 1)
                over_tiles(act, first, second, behind=False)
                if x_out is not None:
                    act.wait_ge(st[0], 5 * 16)
                    act.wait_ge(st[1], 4 * 16)

            @block.vector
            def _(dve):
                def first(t, p, n):
                    r = rows(t)
                    if kt:
                        dve.wait_ge(y_done, t + 1)
                        dve.wait_ge(x_ld[p], n * 16 + 16)
                        dve.tensor_tensor(xS[p][0:r, :], xS[p][0:r, :], Y[p][0:r, :], ALU.add).then_inc(x_new, 1)
                    if gain is None:
                        return
                    dve.wait_ge(root, t + 1)
                    if not (isinstance(t, int) and t < 2):
                        dve.wait_ge(scaled, t - 1)
                    dve.reciprocal(ss[0:r, p, 2:3], ss[0:r, p, 1:2]).then_inc(rstd, 1)

                def second(t, p, n):
                    if gain is None:
                        return
                    r = rows(t)
                    dve.wait_ge(turned, t + 1)
                    cols = slice(NP, NTOK) if r == NS else ds(t * 128, 128)
                    dve.tensor_tensor(hT[:, :, cols], TP[p][:, :, 0:r], g[:, :].unsqueeze(2).broadcast_to([128, KD, r]),
                                      ALU.mult).then_inc(h_out, 1)

                dve.memset(ss[:, :, :], 0.0).then_inc(cleared, 1)
                if gain is not None:
                    dve.wait_ge(g_ld, 16)
                over_tiles(dve, first, second)


def gdn_setup(nc, ident, hT, w_in, conv_w, conv_state, a_log, dt_bias, onorm_g, state_in,
              gate_rows, taps, tok, sall, onorm, causal, level, lnq):
    with ExitStack() as ctx:
        def sb(name, shape):
            return ctx.enter_context(nc.sbuf_tensor("gs_" + name, shape, F32))

        sem = semaphores(nc, ctx, "gs_")

        wab = sb("wab", [128, KD, 2 * H_A])
        raw7 = sb("raw7", [7, 3 * 1024])
        alog, dtb = sb("alog", [H_A, 1]), sb("dtb", [H_A, 1])
        y, e, sp_, b = sb("y", [H_A, PAD]), sb("e", [H_A, PAD]), sb("sp", [H_A, PAD]), sb("b", [H_A, PAD])
        beta, G, nbeg, egl = sb("beta", [H_A, PAD]), sb("G", [H_A, PAD]), sb("nbeg", [H_A, PAD]), sb("egl", [H_A, PAD])
        fresh = sb("fresh", [H_A, PAD])
        ab = ctx.enter_context(nc.psum_tensor("gs_ab", [H_A, 2, 3, 512], F32))
        pt = ctx.enter_context(nc.psum_tensor("gs_pt", [128, 512], F32))
        px = ctx.enter_context(nc.psum_tensor("gs_px", [128, 512], F32))

        ld_w, ld_small, ld_raw, ld_state = sem("ld_w"), sem("ld_small"), sem("ld_raw"), sem("ld_state")
        cleared, ab_done, taps_done, a_step, d_step = sem("cleared"), sem("ab_done"), sem("taps_done"), sem("a_step"), sem("d_step")
        p_step, tok_done, st = sem("p_step"), sem("tok_done"), sem("st")

        with nc.Block() as block:
            @block.sync
            def _(sp):
                sp.dma_start(wab[:, :, :], w_in.rearrange("(k p) n -> p k n", p=128)[:, :, 3072:3072 + 2 * H_A]).then_inc(ld_w, 16)
                sp.dma_start(alog[:, :], a_log.unsqueeze(1)).then_inc(ld_small, 16)
                sp.dma_start(dtb[:, :], dt_bias.unsqueeze(1)).then_inc(ld_small, 16)
                sp.dma_start(onorm[:, :], onorm_g.unsqueeze(1)).then_inc(ld_small, 16)
                sp.dma_start(raw7[0:4, :], conv_w).then_inc(ld_raw, 16)
                sp.dma_start(raw7[4:7, :], conv_state).then_inc(ld_raw, 16)
                sp.dma_start(sall[:, :, :], state_in.rearrange("h d v -> d h v")).then_inc(ld_state, 16)
                sp.wait_ge(ld_state, 16)
                sp.wait_ge(d_step, 8)
                sp.dma_start(gate_rows[0], G[:, :]).then_inc(st, 16)
                sp.dma_start(gate_rows[1], beta[:, :]).then_inc(st, 16)
                sp.wait_ge(st, 32)

            @block.tensor
            def _(pe):
                pe.wait_ge(ld_w, 16)
                for q in range(2):
                    for c, (c0, w) in enumerate(BANKS):
                        for k in range(KD):
                            mm = pe.matmul(ab[:, q, c, 0:w], wab[:, k, H_A * q:H_A * q + H_A], hT[:, k, c0:c0 + w],
                                           start=k == 0, stop=k == KD - 1)
                    mm.then_inc(ab_done, 1)
                pe.wait_ge(ld_raw, 32)
                for n in range(24):
                    mm = pe.transpose(pt[:, 7 * n:7 * n + 7], raw7[:, 128 * n:128 * n + 128], ident[0:7, 0:7])
                mm.then_inc(taps_done, 1)
                pe.wait_ge(d_step, 8)
                for q, row in enumerate((G, beta, nbeg, egl)):
                    for t in range(TILES):
                        c = (q * TILES + t) * H_A
                        mm = pe.transpose(px[:, c:c + H_A], row[:, 128 * t:128 * t + 128], ident[0:H_A, 0:H_A])
                mm.then_inc(tok_done, 1)

            @block.scalar
            def _(act):
                act.preload_act_table_set("natural_log_exp_and_others")
                act.wait_ge(ld_small, 48)
                act.activation(alog[:, :], alog[:, :], ACT.Exp).then_inc(a_step, 1)
                act.wait_ge(ab_done, 2)
                act.activation(y[:, 0:NTOK], ab[:, 0, :, :].rearrange("p c n -> p (c n)")[:, 0:NTOK], ACT.Identity,
                               bias=dtb[:, 0:1]).then_inc(a_step, 1)
                act.wait_ge(a_step, 2)
                act.activation(e[:, 0:NTOK], y[:, 0:NTOK], ACT.Abs).then_inc(a_step, 1)
                act.wait_ge(a_step, 3)
                act.activation(e[:, 0:NTOK], e[:, 0:NTOK], ACT.Exp, scale=-1.0).then_inc(a_step, 1)
                act.wait_ge(a_step, 4)
                act.activation(e[:, 0:NTOK], e[:, 0:NTOK], ACT.Ln, bias=1.0).then_inc(a_step, 1)
                act.activation(b[:, 0:NTOK], ab[:, 1, :, :].rearrange("p c n -> p (c n)")[:, 0:NTOK], ACT.Exp,
                               scale=-1.0).then_inc(a_step, 1)
                act.wait_ge(a_step, 6)
                act.activation(b[:, 0:NTOK], b[:, 0:NTOK], ACT.Ln, bias=1.0).then_inc(a_step, 1)
                act.wait_ge(a_step, 7)
                act.activation(beta[:, 0:NTOK], b[:, 0:NTOK], ACT.Exp, scale=-1.0).then_inc(a_step, 1)
                act.wait_ge(d_step, 6)
                act.activation(nbeg[:, :], G[:, :], ACT.Exp).then_inc(a_step, 1)
                act.wait_ge(d_step, 7)
                act.activation(egl[:, :], egl[:, :], ACT.Exp).then_inc(a_step, 1)

            @block.vector
            def _(dve):
                n = [0]

                def step(ins):
                    n[0] += 1
                    ins.then_inc(d_step, 1)
                    dve.wait_ge(d_step, n[0])

                dve.wait_ge(taps_done, 1)
                step(dve.tensor_copy(taps[:, :, :], pt[:, 0:168].rearrange("p (n s) -> p n s", s=7)))
                dve.wait_ge(cleared, 2)
                dve.wait_ge(a_step, 5)
                step(dve.scalar_tensor_tensor(sp_[:, 0:NTOK], y[:, 0:NTOK], 0.0, e[:, 0:NTOK], ALU.max, ALU.add))
                step(dve.tensor_scalar(sp_[:, 0:NTOK], sp_[:, 0:NTOK], alog[:, 0:1], -1.0, ALU.mult, ALU.mult))
                step(dve.tensor_tensor_scan(G[:, 0:CW], fresh[:, 0:CW], sp_[:, 0:CW], 0.0, ALU.mult, ALU.add))
                step(dve.memset(G[:, CW:PAD], 0.0))
                last = G[:, :].rearrange("p (c n) -> p c n", n=CHUNK)[:, :, CHUNK - 1:CHUNK].broadcast_to([H_A, PAD // CHUNK, CHUNK])
                step(dve.memset(lnq[:, :], -0.5 * math.log(128.0)))
                step(dve.tensor_tensor(egl[:, :].rearrange("p (c n) -> p c n", n=CHUNK), last,
                                       G[:, :].rearrange("p (c n) -> p c n", n=CHUNK), ALU.subtract))
                dve.wait_ge(a_step, 10)
                step(dve.scalar_tensor_tensor(nbeg[:, :], nbeg[:, :], -1.0, beta[:, :], ALU.mult, ALU.mult))
                dve.wait_ge(tok_done, 1)
                step(dve.tensor_copy(tok[:, :, :, :].rearrange("p h q t -> p q t h"),
                                     px[:, 0:4 * TILES * H_A].rearrange("p (q t h) -> p q t h", q=4, t=TILES)))

            @block.gpsimd
            def _(pool):
                pool.memset(sp_[:, NTOK:PAD], 0.0)
                pool.memset(beta[:, NTOK:PAD], 0.0)
                pool.memset(fresh[:, :], 1.0).then_inc(cleared, 1)
                pool.wait_ge(cleared, 1)
                pool.memset(fresh[:, :].rearrange("p (c n) -> p c n", n=CHUNK)[:, :, 0:1], 0.0).then_inc(cleared, 1)
                pool.memset(causal[:, :], 0.0).then_inc(p_step, 1)
                pool.memset(level[:, :, :], 0.0).then_inc(p_step, 1)
                pool.wait_ge(p_step, 2)
                pool.affine_select(out=causal[:, :], in_=causal[:, :], compare_op=ALU.is_ge, fill=NEG, base=0,
                                   pattern=[[1, 128]], channel_multiplier=-1).then_inc(p_step, 1)
                for l in range(LEVELS):
                    v = level[:, l, :].rearrange("p (b u r) -> p b u r", u=2, r=1 << l)[:, :, 1, :]
                    pool.memset(v, 1.0).then_inc(p_step, 1)
                pool.wait_ge(p_step, 3 + LEVELS)
                pool.memset(causal[0:CHUNK, CHUNK:128], NEG).then_inc(p_step, 1)
                for l in range(LEVELS):
                    s, nb = 1 << l, 64 >> l
                    v = level[:, l, :].rearrange("p (b u r) -> p b u r", u=2, r=s)[:, :, 1, :]
                    pool.affine_select(out=v, in_=v, compare_op=ALU.is_ge, fill=0.0, base=0,
                                       pattern=[[-2 * s, nb], [0, s]], channel_multiplier=1).then_inc(p_step, 1)
                    pool.wait_ge(p_step, 5 + LEVELS + 2 * l)
                    pool.affine_select(out=v, in_=v, compare_op=ALU.is_ge, fill=0.0, base=s - 1,
                                       pattern=[[2 * s, nb], [0, s]], channel_multiplier=-1).then_inc(p_step, 1)


H_A = 8
GC = 384
LEVELS = 6


GDN_ORDER = [3, 0, 1, 2]
GDN_COL = [0, 1024, 2048, 3088]


def gdn_weights(W, w_ld, w_in):
    w_cols = w_in.rearrange("(k p) n -> p k n", p=128)
    return [(W[:, j, :, :], w_cols[:, :, GDN_COL[j]:GDN_COL[j] + 128], w_ld[j]) for j in GDN_ORDER]


def gdn(nc, ident, ones, eps, hT, W, w_ld, w_in, conv_w, conv_state, a_log, dt_bias, onorm_g, state_in,
        gate_rows, o_dram, conv_p, conv_s, state_p, state_s, ahead):
    with ExitStack() as ctx:
        def sb(name, shape):
            return ctx.enter_context(nc.sbuf_tensor("gdn_" + name, shape, F32))

        sem = semaphores(nc, ctx, "gdn_")

        taps = sb("taps", [128, 24, 7])
        tok = sb("tok", [128, H_A, 4, TILES])
        sall = sb("sall", [128, H_A, 128])
        onorm = sb("onorm", [128, 1])
        causal = sb("causal", [128, 128])
        level = sb("level", [128, LEVELS, 128])
        lnq = sb("lnq", [128, 1])
        gdn_setup(nc, ident, hT, w_in, conv_w, conv_state, a_log, dt_bias, onorm_g, state_in,
                  gate_rows, taps, tok, sall, onorm, causal, level, lnq)

        U = sb("U", [128, 3, 3 + NP + 3 + CHUNK])
        zraw = sb("zraw", [128, NTOK])
        conv = sb("conv", [128, 3, NP + 3 + CHUNK])
        act3 = sb("act3", [128, 3, PAD])
        zs = sb("zs", [128, NTOK])
        sq = sb("sq", [128, 2, CW])
        rs = sb("rs", [128, 2, CW])
        KN = sb("KN", [128, PAD])
        QN = sb("QN", [128, PAD])
        KB = sb("KB", [128, PAD])
        QG = sb("QG", [128, PAD])
        GB = sb("GB", [128, PAD])
        BB = sb("BB", [128, PAD])
        EG = sb("EG", [128, CW])
        dec = sb("dec", [128, TILES, 128])
        AT = sb("AT", [128, TILES, 128])
        QK = sb("QK", [128, TILES, 128])
        TT = sb("TT", [128, TILES, 128])
        TM = sb("TM", [128, TILES, 128])
        BT = sb("BT", [128, TILES, 128])
        VV = sb("VV", [128, TILES, 128])
        KT = sb("KT", [128, TILES, 128])
        VB = sb("VB", [128, TILES, 128])
        R = sb("R", [128, 128])
        Ub = sb("Ub", [128, 128])
        S = sb("S", [128, 2, 128])
        Ss = sb("Ss", [128, 128])
        Sn = sb("Sn", [128, 128])
        OF = sb("OF", [128, CW])
        cwc = sb("cwc", [128, 3, 7])
        cur = sb("cur", [128, 4, TILES])
        tails = sb("tails", [128, 18])
        tailsT = sb("tailsT", [18, 128])

        pj = ctx.enter_context(nc.psum_tensor("gdn_pj", [128, 2, 512], F32))
        P3 = ctx.enter_context(nc.psum_tensor("gdn_P3", [128, 3, 512], F32))
        X3 = ctx.enter_context(nc.psum_tensor("gdn_X3", [128, 3, 512], F32))
        P3f = P3[:, :, :].rearrange("p b n -> p (b n)")
        X3f = X3[:, :, :].rearrange("p b n -> p (b n)")

        gb_ld = sem("gb_ld")
        proj_done, proj_out = sem("proj_done"), sem("proj_out")
        padded, params, conv_step, tails_ok = sem("padded"), sem("params"), sem("conv_step"), sem("tails_ok")
        silu_z, silu, squared = sem("silu_z"), sem("silu"), sem("squared")
        sums, lns, rsq = sem("sums"), sem("lns"), sem("rsq")
        normed, beta_keys, gated_q, eg_ok = sem("normed"), sem("beta_keys"), sem("gated_q"), sem("eg_ok")
        diffs, dec_ok = sem("diffs"), sem("dec_ok")
        kk_done, qk_done, at_ok, qk_ok = sem("kk_done"), sem("qk_done"), sem("at_ok"), sem("qk_ok")
        masked, tt_ok, tm_ok = sem("masked"), sem("tt_ok"), sem("tm_ok")
        v_done, v_out, x_done = sem("v_done"), sem("v_out"), sem("x_done")
        turned, turned_out = sem("turned"), sem("turned_out")
        s_zero, ss_ok, ks_done, r_ok = sem("s_zero"), sem("ss_ok"), sem("ks_done"), sem("r_ok")
        u_done, u_ok, su_done, s_ok, o_done = sem("u_done"), sem("u_ok"), sem("su_done"), sem("s_ok"), sem("o_done")
        o_sq, o_raw, o_sum, o_rs, o_fin = sem("o_sq"), sem("o_raw"), sem("o_sum"), sem("o_rs"), sem("o_fin")
        st_tail, st_p, st_s, st_o = sem("st_tail"), sem("st_p"), sem("st_s"), sem("st_o")

        ORDER, COL = GDN_ORDER, GDN_COL
        w_cols = w_in.rearrange("(k p) n -> p k n", p=128)
        GROUP = [(0, 3), (3, 3), (6, 3)]

        FILL, PER_LEVEL, LEAN = (28, 16, 6), 2, ()

        def chunk_steps(c):
            return sum(FILL) + PER_LEVEL * (LEVELS - 1) + 2 * c - sum(x < c for x in LEAN)

        def g3(buf, g):
            return buf[:, 3 * g:3 * g + 3, :]

        def p3(bank, g):
            return bank[:, g, 0:GC].rearrange("p (t n) -> p t n", t=3)

        def chunk(c):
            t, a = (c // 2, c % 2)
            return t, a, slice(64 * a, 64 * a + 64)

        with nc.Block() as block:
            @block.sync
            def _(sp):
                def load_w(n, j, col):
                    sp.dma_start(W[:, j, :, :], w_cols[:, :, ds(col, 128)]).then_inc(w_ld[j], 16)

                def load_gates(n):
                    sp.dma_start(GB[:, 0:CW], gate_rows[0, ds(n, 1), 0:CW].to_broadcast([128, CW])).then_inc(gb_ld, 16)
                    sp.dma_start(BB[:, 0:CW], gate_rows[1, ds(n, 1), 0:CW].to_broadcast([128, CW])).then_inc(gb_ld, 16)

                sp.wait_ge(padded, 1)
                load_gates(0)
                with sp.Fori(0, H_A - 1) as h:
                    for p, j in enumerate(ORDER):
                        sp.wait_ge(proj_done, h * 12 + 3 * p + 3)
                        load_w(h + 1, j, h * 128 + 128 + COL[j])
                    sp.wait_ge(eg_ok, h + 1)
                    sp.wait_ge(beta_keys, h + 1)
                    sp.wait_ge(diffs, h * TILES + TILES)
                    load_gates(h + 1)
                sp.wait_ge(proj_done, H_A * 12)
                load_ahead(sp, ahead)

            @block.tensor
            def _(pe):
                def project(n):
                    m = 0
                    for p, j in enumerate(ORDER):
                        wait(pe, w_ld[j], n * 16 + 16)
                        for c0, w in JOBS:
                            wait(pe, proj_out, n * 12 + (m - 1))
                            for k in range(KD):
                                mm = pe.matmul(pj[:, m % 2, 0:w], W[:, j, k, :], hT[:, k, c0:c0 + w],
                                               start=k == 0, stop=k == KD - 1)
                                if k == KD - 1:
                                    mm.then_inc(proj_done, 1)
                                yield
                            m += 1

                def head(h, more):
                    steps = project(h + 1) if more else iter(())

                    def fill(n):
                        for _ in range(n):
                            next(steps, None)

                    fill(FILL[0])
                    for x, bank in enumerate((P3, X3)):
                        pe.wait_ge(squared, h * 2 + x + 1)
                        if x == 0:
                            wait(pe, o_raw, h * 1)
                        else:
                            wait(pe, o_rs, h * 2)
                        for b, w in ((0, 512), (1, 512), (2, CW - 1024)):
                            mm = pe.matmul(bank[:, b, 0:w], ones[:, :], sq[:, x, 512 * b:512 * b + w],
                                           start=True, stop=True)
                        mm.then_inc(sums, 1)
                    fill(FILL[1])
                    pe.wait_ge(beta_keys, h + 1)
                    pe.wait_ge(lns, h * 2 + 2)
                    for g in range(3):
                        for t in range(3 * g, 3 * g + 3):
                            c = 128 * t
                            mm = pe.matmul(P3[:, g, 128 * (t - 3 * g):128 * (t - 3 * g) + 128], KN[:, c:c + 128],
                                           KB[:, c:c + 128], start=True, stop=True)
                        mm.then_inc(kk_done, 1)
                    for g in range(3):
                        for t in range(3 * g, 3 * g + 3):
                            c = 128 * t
                            mm = pe.matmul(X3[:, g, 128 * (t - 3 * g):128 * (t - 3 * g) + 128], KN[:, c:c + 128],
                                           QN[:, c:c + 128], start=True, stop=True)
                        mm.then_inc(qk_done, 1)
                    fill(FILL[2])
                    for x, src in enumerate((KN, act3[:, 2, :])):
                        for g in range(3):
                            if x == 0:
                                pe.wait_ge(qk_ok, h * 3 + g + 1)
                            else:
                                pe.wait_ge(turned_out, h * 7 + g + 1)
                                if g == 0:
                                    pe.wait_ge(silu, h * 6 + 6)
                            for t in range(3):
                                c = 384 * g + 128 * t
                                mm = pe.transpose(X3[:, g, 128 * t:128 * t + 128], src[:, c:c + 128], ident[:, :])
                            if x == 1 and g == 2:
                                pe.wait_ge(tails_ok, h * 2 + 2)
                                mm.then_inc(turned, 1)
                                mm = pe.transpose(X3[0:18, g, GC:GC + 128], tails[:, :], ident[:, :])
                            mm.then_inc(turned, 1)
                    for l in range(1, LEVELS):
                        for g in range(3):
                            pe.wait_ge(masked, h * 18 + 3 * l + g + 1)
                            pe.wait_ge(tm_ok, h * 15 + 3 * (l - 1) + g + 1)
                            for t in range(3):
                                mm = pe.matmul(P3[:, g, 128 * t:128 * t + 128], BT[:, 3 * g + t, :], TM[:, 3 * g + t, :],
                                               start=True, stop=True)
                            mm.then_inc(v_done, 1)
                        fill(1)
                        for g in range(3):
                            pe.wait_ge(v_out, h * 15 + 3 * (l - 1) + g + 1)
                            if l == 1:
                                pe.wait_ge(turned_out, h * 7 + (7 if g == 2 else 4 + g))
                            for t in range(3):
                                mm = pe.matmul(X3[:, g, 128 * t:128 * t + 128], VV[:, 3 * g + t, :], TT[:, 3 * g + t, :],
                                               start=True, stop=True)
                            mm.then_inc(x_done, 1)
                        fill(PER_LEVEL - 1)
                    pe.wait_ge(gated_q, h + 1)
                    pe.wait_ge(ss_ok, h + 1)
                    pe.wait_ge(tt_ok, h * 18 + 18)
                    for c in range(NCH + 1):
                        t, a, P = chunk(c)
                        state = S[:, c % 2, :] if c < NCH else Ss[:, :]
                        if c == 0:
                            pe.wait_ge(s_zero, h + 1)
                        elif c < NCH:
                            pe.wait_ge(s_ok, h * 17 + c)
                        if c:
                            pe.wait_ge(r_ok, h * 17 + c)
                        pe.matmul(X3[P, 0, 0:128], KN[:, 64 * c:64 * c + 64], state, start=True, stop=True).then_inc(ks_done, 1)
                        if c not in LEAN:
                            fill(1)
                        pe.wait_ge(r_ok, h * 17 + c + 1)
                        if c:
                            pe.wait_ge(u_ok, h * 17 + c)
                        pe.matmul(X3[:, 1, 0:128], TT[P, t, :], R[P, :], start=True, stop=True).then_inc(u_done, 1)
                        fill(1)
                        pe.wait_ge(u_ok, h * 17 + c + 1)
                        if c:
                            pe.wait_ge(s_ok, h * 17 + c)
                        pe.matmul(X3[:, 2, 0:128], KT[P, t, :], Ub[P, :], start=True, stop=True).then_inc(su_done, 1)
                        o = P3f[:, 64 * c:64 * c + 64]
                        pe.matmul(o, state, QG[:, 64 * c:64 * c + 64], start=True, stop=False)
                        pe.matmul(o, Ub[P, :], QK[P, t, 64 * a:64 * a + 64], start=False, stop=True).then_inc(o_done, 1)
                    for _ in steps:
                        pass
                    pe.wait_ge(o_sq, h + 1)
                    for b, w in ((0, 512), (1, 512), (2, CW - 1024)):
                        if b == 0:
                            pe.wait_ge(r_ok, h * 17 + 17)
                            pe.wait_ge(s_ok, h * 17 + 17)
                        mm = pe.matmul(X3[:, b, 0:w], ones[:, :], sq[:, 0, 512 * b:512 * b + w], start=True, stop=True)
                    mm.then_inc(o_sum, 1)

                pe.wait_ge(padded, 1)
                for _ in project(0):
                    pass
                head(0, True)
                with pe.Fori(1, H_A - 1) as h:
                    head(h, True)
                head(H_A - 1, False)

            @block.scalar
            def _(act):
                def proj_copy(n, ms):
                    for m in ms:
                        j, (c0, w) = ORDER[m // 3], JOBS[m % 3]
                        act.wait_ge(proj_done, n * 12 + m + 1)
                        if j == 3:
                            wait(act, silu_z, n * 1)
                            dst = zraw[:, c0:c0 + w]
                        else:
                            wait(act, conv_step, n * 12 - 8 + 4 * j)
                            wait(act, tails_ok, n * 2)
                            dst = U[:, j, 3 + c0:3 + c0 + w]
                            if c0 + w > NP:
                                w = NP - c0
                                act.activation(dst[:, 0:w], pj[:, m % 2, 0:w], ACT.Copy)
                                dst = U[:, j, 6 + NP:6 + NTOK]
                                act.activation(dst, pj[:, m % 2, w:w + NS], ACT.Copy).then_inc(proj_out, 1)
                                continue
                        act.activation(dst, pj[:, m % 2, 0:w], ACT.Copy).then_inc(proj_out, 1)

                def head(h, more):
                    left = list(range(12)) if more else []

                    def jobs(steps):
                        while left and 8 * (left[0] + 1) <= steps:
                            proj_copy(h + 1, [left.pop(0)])

                    act.wait_ge(proj_out, h * 12 + 3)
                    wait(act, o_fin, h * 3)
                    act.activation(zs[:, :], zraw[:, :], ACT.Silu).then_inc(silu_z, 1)
                    jobs(8)
                    for j in range(3):
                        act.wait_ge(conv_step, h * 12 + 4 * j + 4)
                        if j < 2:
                            wait(act, normed, h * 2)
                        else:
                            wait(act, turned, h * 7)
                        act.activation(act3[:, j, 0:NP], conv[:, j, 0:NP], ACT.Silu).then_inc(silu, 1)
                        act.activation(act3[:, j, NP:CW], conv[:, j, NP + 3:], ACT.Silu).then_inc(silu, 1)
                        if j < 2:
                            act.wait_ge(silu, h * 6 + 2 * j + 2)
                            if j == 0:
                                wait(act, o_sum, h * 1)
                            act.activation(sq[:, j, :], act3[:, j, 0:CW], ACT.Square).then_inc(squared, 1)
                        jobs(min(FILL[0], 8 * j + 16))
                    act.preload_act_table_set("natural_log_exp_and_others")
                    act.wait_ge(gb_ld, h * 32 + 32)
                    wait(act, s_ok, h * 17)
                    wait(act, gated_q, h * 1)
                    act.activation(EG[:, :], GB[:, 0:CW], ACT.Exp).then_inc(eg_ok, 1)
                    for x, bank in enumerate((P3f, X3f)):
                        act.wait_ge(sums, h * 2 + x + 1)
                        wait(act, normed, h * 2)
                        if x == 0:
                            wait(act, o_fin, h * 3)
                        act.activation(rs[:, x, :], bank[:, 0:CW], ACT.Ln, bias=eps[:, 0:1]).then_inc(lns, 1)
                        act.wait_ge(lns, h * 2 + x + 1)
                        act.activation(rs[:, x, :], rs[:, x, :], ACT.Exp, scale=-0.5,
                                       bias=lnq[:, 0:1] if x == 0 else 0.0).then_inc(rsq, 1)
                    jobs(FILL[0] + FILL[1])
                    for g in range(3):
                        act.wait_ge(diffs, h * TILES + 3 * g + 3)
                        act.activation(g3(dec, g), g3(dec, g), ACT.Exp).then_inc(dec_ok, 1)
                    jobs(FILL[0] + FILL[1] + FILL[2])
                    for l in range(1, LEVELS):
                        for g in range(3):
                            act.wait_ge(v_done, h * 15 + 3 * (l - 1) + g + 1)
                            if l > 1:
                                act.wait_ge(x_done, h * 15 + 3 * (l - 2) + g + 1)
                            else:
                                wait(act, x_done, h * 15)
                            act.activation(g3(VV, g), p3(P3, g), ACT.Copy).then_inc(v_out, 1)
                        jobs(FILL[0] + FILL[1] + FILL[2] + PER_LEVEL * (l - 1))
                    for c in range(NCH + 1):
                        t, a, P = chunk(c)
                        act.wait_ge(u_done, h * 17 + c + 1)
                        if c > 1:
                            act.wait_ge(o_done, h * 17 + c - 1)
                        else:
                            wait(act, o_done, h * 17)
                        act.activation(Ub[P, :], X3[P, 1, 0:128], ACT.Copy).then_inc(u_ok, 1)
                        jobs(chunk_steps(c))
                    act.wait_ge(o_done, h * 17 + 17)
                    act.activation(sq[:, 0, :], P3f[:, 0:CW], ACT.Square).then_inc(o_sq, 1)
                    wait(act, st_o, h * 32)
                    act.activation(OF[:, :], P3f[:, 0:CW], ACT.Copy).then_inc(o_raw, 1)
                    jobs(96)
                    act.wait_ge(o_sum, h + 1)
                    act.activation(rs[:, 0, :], X3f[:, 0:CW], ACT.Ln, scale=1.0 / 128, bias=eps[:, 0:1]).then_inc(o_rs, 1)
                    act.wait_ge(o_rs, h * 2 + 1)
                    act.activation(rs[:, 0, :], rs[:, 0, :], ACT.Exp, scale=-0.5).then_inc(o_rs, 1)
                    hd = h if isinstance(h, int) else act.snap(h)
                    act.wait_ge(turned_out, h * 7 + 7)
                    for j in range(3):
                        col = h * 128 + 1024 * j
                        act.dma_start(conv_p[:, ds(col, 128)], tailsT[3 * j:3 * j + 3, :]).then_inc(st_tail, 16)
                        act.dma_start(conv_s[:, ds(col, 128)], tailsT[9 + 3 * j:12 + 3 * j, :]).then_inc(st_tail, 16)
                    act.wait_ge(s_ok, h * 17 + 17)
                    act.dma_start(state_p[ds(h, 1), :, :].rearrange("o d v -> d (o v)"), S[:, 0, :]).then_inc(st_p, 16)
                    act.dma_start(state_s[ds(h, 1), :, :].rearrange("o d v -> d (o v)"), Sn[:, :]).then_inc(st_s, 16)
                    act.wait_ge(o_fin, h * 3 + 3)
                    act.dma_start(o_dram[ds(h * 128, 128), 0:NP], OF[:, 0:NP]).then_inc(st_o, 16)
                    act.dma_start(o_dram[ds(h * 128, 128), NP:NTOK], OF[:, NP:NTOK]).then_inc(st_o, 16)

                proj_copy(0, range(12))
                head(0, True)
                with act.Fori(1, H_A - 1) as h:
                    head(h, True)
                head(H_A - 1, False)
                act.wait_ge(st_tail, H_A * 96)
                act.wait_ge(st_p, H_A * 16)
                act.wait_ge(st_s, H_A * 16)
                act.wait_ge(st_o, H_A * 32)

            @block.vector
            def _(dve):
                def head(h):
                    wait(dve, params, h * 3)
                    dve.tensor_copy(cwc[:, :, :], taps[:, :, :].rearrange("p (j h) s -> p h j s", j=3)[:, ds(h, 1), :, :]
                                    .rearrange("p o j s -> p (o j) s")).then_inc(params, 1)
                    wait(dve, r_ok, h * 17)
                    wait(dve, turned_out, h * 7)
                    dve.tensor_copy(cur[:, :, :], tok[:, ds(h, 1), :, :].rearrange("p o q t -> p (o q) t")).then_inc(params, 1)
                    dve.wait_ge(params, h * 3 + 1)
                    wait(dve, conv_step, h * 12)
                    dve.tensor_copy(U[:, :, NP + 3:NP + 6], cwc[:, :, 4:7]).then_inc(params, 1)
                    wait(dve, st_p, h * 16)
                    dve.memset(S[:, 0, :], 0.0).then_inc(s_zero, 1)
                    wait(dve, turned, h * 7)
                    dve.wait_ge(proj_out, h * 12 + 12)
                    tv = tails[:, :].rearrange("p (k j r) -> p k j r", k=2, j=3)
                    dve.tensor_copy(tv[:, 0, :, :], U[:, :, NP:NP + 3]).then_inc(tails_ok, 1)
                    dve.tensor_copy(tv[:, 1, :, :], U[:, :, NP + 3 + NS:NP + 6 + NS]).then_inc(tails_ok, 1)
                    dve.wait_ge(params, h * 3 + 3)
                    n = NP + 3 + CHUNK
                    wait(dve, silu, h * 6)
                    for j in range(3):
                        dve.tensor_scalar(conv[:, j, :], U[:, j, 0:n], cwc[:, j, 0:1], None, ALU.mult).then_inc(conv_step, 1)
                        for k in range(1, 4):
                            dve.wait_ge(conv_step, h * 12 + 4 * j + k)
                            dve.scalar_tensor_tensor(conv[:, j, :], U[:, j, k:k + n], cwc[:, j, k:k + 1], conv[:, j, :],
                                                     ALU.mult, ALU.add).then_inc(conv_step, 1)
                    dve.wait_ge(gb_ld, h * 32 + 32)
                    wait(dve, qk_ok, h * 3)
                    wait(dve, at_ok, h * 3)
                    for t in range(TILES):
                        dve.scalar_tensor_tensor(dec[:, t, :], GB[:, 128 * t:128 * t + 128], cur[:, 0, t:t + 1], causal[:, :],
                                                 ALU.subtract, ALU.add).then_inc(diffs, 1)
                    for x, dst in enumerate((QN, KN)):
                        dve.wait_ge(rsq, h * 2 + x + 1)
                        dve.wait_ge(silu, h * 6 + 2 * x + 2)
                        if x == 0:
                            wait(dve, gated_q, h * 1)
                            wait(dve, qk_done, h * 3)
                        else:
                            wait(dve, ks_done, h * 17)
                        dve.tensor_tensor(dst[:, 0:CW], act3[:, x, 0:CW], rs[:, x, :], ALU.mult).then_inc(normed, 1)
                    for g in range(3):
                        dve.wait_ge(kk_done, h * 3 + g + 1)
                        dve.wait_ge(dec_ok, h * 3 + g + 1)
                        wait(dve, masked, h * 18)
                        dve.tensor_tensor(g3(AT, g), p3(P3, g), g3(dec, g), ALU.mult).then_inc(at_ok, 1)
                    for g in range(3):
                        dve.wait_ge(qk_done, h * 3 + g + 1)
                        wait(dve, o_done, h * 17)
                        dve.tensor_tensor(g3(QK, g), p3(X3, g), g3(dec, g), ALU.mult).then_inc(qk_ok, 1)
                    eye = ident[:, :].unsqueeze(1).broadcast_to([128, 3, 128])
                    for g in range(3):
                        dve.wait_ge(masked, h * 18 + g + 1)
                        wait(dve, u_done, h * 17)
                        dve.tensor_tensor(g3(TT, g), eye, g3(BT, g), ALU.subtract).then_inc(tt_ok, 1)
                    for g in range(3):
                        dve.wait_ge(tt_ok, h * 18 + g + 1)
                        wait(dve, v_done, h * 15)
                        dve.transpose(g3(TM, g), g3(TT, g)).then_inc(tm_ok, 1)
                    for x, (dst, q) in enumerate(((KT, 3), (VB, 1))):
                        for g in range(3):
                            dve.wait_ge(turned, h * 7 + (7 if x == 1 and g == 2 else 3 * x + g + 1))
                            if x == 0:
                                wait(dve, su_done, h * 17)
                            else:
                                wait(dve, r_ok, h * 17)
                            by_token = cur[:, q, 3 * g:3 * g + 3].unsqueeze(2).broadcast_to([128, 3, 128])
                            dve.tensor_tensor(g3(dst, g), p3(X3, g), by_token, ALU.mult).then_inc(turned_out, 1)
                    dve.wait_ge(turned, h * 7 + 7)
                    wait(dve, st_tail, h * 96)
                    dve.tensor_copy(tailsT[:, :], X3[0:18, 2, GC:GC + 128]).then_inc(turned_out, 1)
                    for l in range(1, LEVELS):
                        for g in range(3):
                            dve.wait_ge(x_done, h * 15 + 3 * (l - 1) + g + 1)
                            dve.tensor_tensor(g3(TT, g), g3(TT, g), p3(X3, g), ALU.subtract).then_inc(tt_ok, 1)
                            if l < LEVELS - 1:
                                dve.wait_ge(tt_ok, h * 18 + 3 * l + g + 1)
                                dve.transpose(g3(TM, g), g3(TT, g)).then_inc(tm_ok, 1)
                    for c in range(NCH + 1):
                        t, a, P = chunk(c)
                        src = S[:, c % 2, :] if c < NCH else Ss[:, :]
                        dst = S[:, (c + 1) % 2, :] if c < NCH else Sn[:, :]
                        dve.wait_ge(ks_done, h * 17 + c + 1)
                        if c > 1:
                            dve.wait_ge(u_done, h * 17 + c - 1)
                        dve.scalar_tensor_tensor(R[P, :], X3[P, 0, 0:128], cur[P, 2, t:t + 1], VB[P, t, :],
                                                 ALU.mult, ALU.add).then_inc(r_ok, 1)
                        dve.wait_ge(su_done, h * 17 + c + 1)
                        if 0 < c < NCH:
                            dve.wait_ge(o_done, h * 17 + c)
                        if c == NCH:
                            wait(dve, st_s, h * 16)
                        if c == 0:
                            dve.wait_ge(s_zero, h + 1)
                        else:
                            dve.wait_ge(s_ok, h * 17 + c)
                        dve.scalar_tensor_tensor(dst, src, EG[:, 64 * c + 63:64 * c + 64], X3[:, 2, 0:128],
                                                 ALU.mult, ALU.add).then_inc(s_ok, 1)
                    dve.wait_ge(o_raw, h + 1)
                    dve.wait_ge(o_rs, h * 2 + 2)
                    dve.tensor_tensor(OF[:, :], OF[:, :], rs[:, 0, :], ALU.mult).then_inc(o_fin, 1)
                    dve.wait_ge(o_fin, h * 3 + 1)
                    dve.wait_ge(silu_z, h + 1)
                    dve.scalar_tensor_tensor(OF[:, 0:NP], OF[:, 0:NP], onorm[:, 0:1], zs[:, 0:NP], ALU.mult, ALU.mult).then_inc(o_fin, 1)
                    dve.scalar_tensor_tensor(OF[:, NP:NTOK], OF[:, NP:NTOK], onorm[:, 0:1], zs[:, NP:NTOK],
                                             ALU.mult, ALU.mult).then_inc(o_fin, 1)

                head(0)
                with dve.Fori(1, H_A - 1) as h:
                    head(h)
                head(H_A - 1)

            @block.gpsimd
            def _(pool):
                for buf in (KN, QN, KB, QG, GB, BB):
                    pool.memset(buf[:, CW:PAD], 0.0)
                pool.memset(act3[:, 2, CW:PAD], 0.0)
                pool.memset(U[:, :, 0:3], 0.0)
                pool.memset(U[:, :, NP + 6 + NS:], 0.0).then_inc(padded, 1)

                def head(h):
                    wait(pool, o_done, h * 17)
                    wait(pool, s_ok, h * 17)
                    pool.tensor_copy(Ss[:, :], sall[:, ds(h, 1), :].rearrange("p o n -> p (o n)")).then_inc(ss_ok, 1)
                    pool.wait_ge(gb_ld, h * 32 + 32)
                    pool.wait_ge(normed, h * 2 + 2)
                    pool.wait_ge(eg_ok, h + 1)
                    wait(pool, kk_done, h * 3)
                    pool.tensor_tensor(KB[:, 0:CW], KN[:, 0:CW], BB[:, 0:CW], ALU.mult).then_inc(beta_keys, 1)
                    for l in range(LEVELS):
                        if l == 1:
                            pool.tensor_tensor(QG[:, 0:CW], QN[:, 0:CW], EG[:, :], ALU.mult).then_inc(gated_q, 1)
                        mask = level[:, l, :].unsqueeze(1).broadcast_to([128, 3, 128])
                        for g in range(3):
                            pool.wait_ge(at_ok, h * 3 + g + 1)
                            if l == 0:
                                wait(pool, v_done, h * 15)
                            elif l == 1:
                                pool.wait_ge(tt_ok, h * 18 + g + 1)
                            else:
                                pool.wait_ge(v_done, h * 15 + 3 * (l - 2) + g + 1)
                            pool.tensor_tensor(g3(BT, g), g3(AT, g), mask, ALU.mult).then_inc(masked, 1)

                head(0)
                with pool.Fori(1, H_A - 1) as h:
                    head(h)
                head(H_A - 1)


B_H, B_D = 16, 64
PAIRS = B_H // 2
SPAN = 5 * 128
REL = 128


BAND_ORDER = [2, 0, 1]
BAND_COL = [4112, 5136, 7184]


def band_weights(W, w_ld, w_in):
    w_cols = w_in.rearrange("(k p) n -> p k n", p=128)
    return [(W[:, j, :, :], w_cols[:, :, BAND_COL[j]:BAND_COL[j] + 128], w_ld[j]) for j in BAND_ORDER]


def band(nc, ident, ones, eps, hT, W, w_ld, w_in, q_g, k_g, rel_bias, cache_k, cache_v, bias_rows,
         o_dram, k_p, v_p, k_s, v_s, ahead):
    ORDER, COL = BAND_ORDER, BAND_COL
    COL_V = 6160
    w_cols = w_in.rearrange("(k p) n -> p k n", p=128)
    with ExitStack() as ctx:
        def sb(n, shape):
            return ctx.enter_context(nc.sbuf_tensor("band_" + n, shape, F32))

        sem = semaphores(nc, ctx, "band_")

        VT = sb("VT", [128, TILES, B_H * B_D])
        VC = sb("VC", [128, 4, B_H * B_D])
        pair_ones = sb("pair_ones", [128, 128])
        g2 = sb("g2", [128, 2])
        lnb = sb("lnb", [128, 1])
        raw = sb("raw", [128, 2, PAD])
        zraw = sb("zraw", [128, PAD])
        pj = ctx.enter_context(nc.psum_tensor("band_pj", [128, 512], F32))
        proj_done, proj_out, z_ok, squared, normed = sem("proj_done"), sem("proj_out"), sem("z_ok"), sem("squared"), sem("normed")

        def load_w(sp, n, j, m):
            sp.dma_start(W[:, j, :, :], w_cols[:, :, ds(n * 128 + (COL[j] + 128 * m), 128)]).then_inc(w_ld[j], 16)

        def project(pe, n):
            m = 0
            for j in ORDER:
                wait(pe, w_ld[j], n * 16 + 16)
                for c0, w in JOBS:
                    wait(pe, proj_out, n * 9 + m)
                    for k in range(KD):
                        mm = pe.matmul(pj[:, 0:w], W[:, j, k, :], hT[:, k, c0:c0 + w], start=k == 0, stop=k == KD - 1)
                        if k == KD - 1:
                            mm.then_inc(proj_done, 1)
                        yield
                    m += 1

        def proj_copy(act, n, m):
            j, (c0, w) = ORDER[m // 3], JOBS[m % 3]
            act.wait_ge(proj_done, n * 9 + m + 1)
            if j == 2:
                wait(act, z_ok, n * 1)
                dst = zraw[:, c0:c0 + w]
            else:
                wait(act, normed, n * 2)
                wait(act, squared, n * 2)
                dst = raw[:, j, c0:c0 + w]
            act.activation(dst, pj[:, 0:w], ACT.Copy).then_inc(proj_out, 1)

        with ExitStack() as sub:
            Wv = sub.enter_context(nc.sbuf_tensor("band_Wv", [128, KD, B_H * B_D], F32))
            rel = sub.enter_context(nc.sbuf_tensor("band_rel", [B_H, 2 * REL + 1], F32))
            vec = sub.enter_context(nc.sbuf_tensor("band_vec", [B_H, 768], F32))
            pv = sub.enter_context(nc.psum_tensor("band_pv", [128, 2, 512], F32))
            wv_ld, rel_ld, c_ld, g_ld = sem("wv_ld"), sem("rel_ld"), sem("c_ld"), sem("g_ld")
            v_done, v_out, vec_ok, st, cleared = sem("v_done"), sem("v_out"), sem("vec_ok"), sem("stv"), sem("cleared")
            QN_, QW = 4, 256

            with nc.Block() as block:
                @block.sync
                def _(sp):
                    sp.dma_start(Wv[:, :, :], w_cols[:, :, COL_V:COL_V + B_H * B_D]).then_inc(wv_ld, 16)
                    sp.dma_start(rel[:, :], rel_bias).then_inc(rel_ld, 16)
                    for x, g in enumerate((q_g, k_g)):
                        for e in range(2):
                            sp.dma_start(g2[64 * e:64 * e + 64, x:x + 1], g.unsqueeze(1)).then_inc(g_ld, 16)
                    sp.dma_start(VC[:, :, :], cache_v.rearrange("(m p) d -> p m d", p=128)).then_inc(c_ld, 16)
                    for p, j in enumerate(ORDER):
                        sp.wait_ge(proj_done, 3 * p + 3)
                        load_w(sp, 0, j, 1)
                    sp.wait_ge(vec_ok, 2)
                    sp.dma_start(bias_rows, vec[:, :]).then_inc(st, 16)
                    sp.wait_ge(v_out, QN_ * TILES)
                    sp.dma_start(v_p.rearrange("(m p) d -> p m d", p=128), VT[:, 4:8, :]).then_inc(st, 16)
                    sp.dma_start(v_s, VT[0:NS, 8, :]).then_inc(st, 16)
                    sp.wait_ge(st, 48)
                    sp.wait_ge(c_ld, 16)
                    sp.wait_ge(g_ld, 64)

                @block.tensor
                def _(pe):
                    for _ in project(pe, 0):
                        pass
                    pe.wait_ge(wv_ld, 16)

                    def quarter(q):
                        for t in range(TILES):
                            wait(pe, v_out, q * TILES + max(t - 1, 0))
                            for k in range(KD):
                                mm = pe.matmul(pv[:, t % 2, 0:QW], hT[:, k, 128 * t:128 * t + 128], Wv[:, k, ds(q * QW, QW)],
                                               start=k == 0, stop=k == KD - 1)
                            mm.then_inc(v_done, 1)

                    quarter(0)
                    with pe.Fori(1, QN_) as q:
                        quarter(q)

                @block.scalar
                def _(act):
                    for m in range(9):
                        proj_copy(act, 0, m)
                    with act.Fori(0, QN_) as q:
                        for t in range(TILES):
                            act.wait_ge(v_done, q * TILES + t + 1)
                            act.activation(VT[:, t, ds(q * QW, QW)], pv[:, t % 2, 0:QW], ACT.Copy).then_inc(v_out, 1)

                @block.vector
                def _(dve):
                    dve.wait_ge(rel_ld, 16)
                    dve.tensor_copy(vec[:, 2 * REL:768], rel[:, 2 * REL:2 * REL + 1].broadcast_to([B_H, 768 - 2 * REL])).then_inc(vec_ok, 1)
                    dve.tensor_copy(vec[:, 0:2 * REL], rel[:, 0:2 * REL]).then_inc(vec_ok, 1)
                    dve.memset(lnb[:, :], -0.5 * math.log(B_D))

                @block.gpsimd
                def _(pool):
                    pool.memset(pair_ones[:, :], 0.0).then_inc(cleared, 1)
                    pool.wait_ge(cleared, 1)
                    pool.memset(pair_ones[0:64, 0:64], 1.0)
                    pool.memset(pair_ones[64:128, 64:128], 1.0)

        zs = sb("zs", [128, PAD])
        sq = sb("sq", [128, 2, PAD])
        rs = sb("rs", [128, 2, PAD])
        QK = sb("QK", [128, 2, PAD])
        ckr = sb("ckr", [128, 4, 128])
        CK = sb("CK", [128, 512])
        stage = sb("stage", [128, 2, SPAN])
        bias = sb("bias", [128, 2, SPAN])
        NS_ = sb("NS", [128, 2, SPAN])
        E = sb("E", [128, 2, SPAN])
        ET = sb("ET", [128, 2, SPAN])
        nm = sb("nm", [128, 18])
        rsum = sb("rsum", [128, 18])
        rinv = sb("rinv", [128, 18])
        OT = sb("OT", [128, 2, 128])
        OF = sb("OF", [128, PAD])
        KO = sb("KO", [128, 5, 128])
        SC = [ctx.enter_context(nc.psum_tensor(f"band_SC{p}", [128, 1024], F32)) for p in range(2)]
        PT = ctx.enter_context(nc.psum_tensor("band_PT", [128, 1024], F32))
        PO = ctx.enter_context(nc.psum_tensor("band_PO", [128, 512], F32))

        ck_ld, b_ld = sem("ck_ld"), sem("b_ld")
        sums, lns, rs_ok = sem("sums"), sem("lns"), sem("rs_ok")
        ko_done, ko_ok, ck_done, ck_ok, bias_ok = sem("ko_done"), sem("ko_ok"), sem("ck_done"), sem("ck_ok"), sem("bias_ok")
        s_done, ns_ok, e_ok, et_done, et_a, et_d = sem("s_done"), sem("ns_ok"), sem("e_ok"), sem("et_done"), sem("et_a"), sem("et_d")
        o_done, ri_ok, o_ok, ot_done, of_ok = sem("o_done"), sem("ri_ok"), sem("o_ok"), sem("ot_done"), sem("of_ok")
        st_k, st_o, mask0 = sem("st_k"), sem("st_o"), sem("mask0")
        unseen = sb("unseen", [128, SPAN])
        junk = sb("junk", [128, 1])
        tick = sb("tick", [128, 18])

        UNITS = 2 * TILES
        LEAD, PER_UNIT = (4, 4, 6), (2, 2, 0)

        def steps_at(u):
            return sum(LEAD) + PER_UNIT[0] * (u + 1) + PER_UNIT[1] * u + PER_UNIT[2] * (u // 2)

        def window(t):
            n = min(t + 1, 5)
            return SPAN - 128 * n, n

        with nc.Block() as block:
            @block.sync
            def _(sp):
                def load_keys(n, m):
                    sp.dma_start(ckr[:, :, :], cache_k.rearrange("(m p) d -> p m d", p=128)[:, :, ds(n * 128 + 128 * m, 128)]).then_inc(ck_ld, 16)

                def load_bias(n, m):
                    for e in range(2):
                        src = bass.AP(tensor=bias_rows.tensor, offset=n * (2 * 768) + (2 * m + e) * 768 + 1, ap=[[1, 128], [1, SPAN]])
                        sp.dma_start(stage[:, e, :], src).then_inc(b_ld, 16)

                load_keys(0, 0)
                load_bias(0, 0)
                sp.wait_ge(ck_done, 1)
                load_keys(0, 1)
                sp.wait_ge(bias_ok, 1)
                load_bias(0, 1)
                with sp.Fori(1, PAIRS - 1) as n:
                    for p, j in enumerate(ORDER):
                        sp.wait_ge(proj_done, n * 9 + 3 * p + 3)
                        load_w(sp, n, j, 1)
                    sp.wait_ge(ck_done, n + 1)
                    load_keys(n, 1)
                    sp.wait_ge(bias_ok, n + 1)
                    load_bias(n, 1)
                sp.wait_ge(proj_done, PAIRS * 9)
                load_ahead(sp, ahead)

            @block.tensor
            def _(pe):
                def pair(n, more):
                    steps = project(pe, n + 1) if more else iter(())

                    def fill(k):
                        for _ in range(k):
                            next(steps, None)

                    fill(LEAD[0])
                    for x in range(2):
                        pe.wait_ge(squared, n * 2 + x + 1)
                        if x == 0:
                            wait(pe, ns_ok, n * UNITS)
                            wait(pe, et_a, n * UNITS)
                            wait(pe, et_d, n * UNITS)
                        for b in range(2):
                            pe.matmul(SC[x][:, 512 * b:512 * b + 512], pair_ones[:, :], sq[:, x, 512 * b:512 * b + 512],
                                      start=True, stop=True)
                        pe.matmul(PT[:, 512 * x:512 * x + NS], pair_ones[:, :], sq[:, x, NP:NTOK],
                                  start=True, stop=True).then_inc(sums, 1)
                    fill(LEAD[1])
                    pe.wait_ge(ck_ld, n * 16 + 16)
                    wait(pe, of_ok, n * TILES)
                    for m in range(4):
                        mm = pe.transpose(PO[:, 128 * m:128 * m + 128], ckr[:, m, :], ident[:, :])
                    mm.then_inc(ck_done, 1)
                    fill(LEAD[2])
                    pe.wait_ge(lns, n * 4 + 4)
                    pe.wait_ge(normed, n * 2 + 2)
                    for m in range(5):
                        w = NS if m == 4 else 128
                        mm = pe.transpose(PT[0:w, 128 * m:128 * m + 128], QK[:, 1, 512 + 128 * m:512 + 128 * m + w], ident[:, :])
                    mm.then_inc(ko_done, 1)
                    pe.wait_ge(ck_ok, n + 1)

                    def scores(u):
                        t, e = u // 2, u % 2
                        F = slice(64 * e, 64 * e + 64)
                        if u >= 2:
                            pe.wait_ge(ns_ok, n * UNITS + u - 1)
                        q = QK[F, 0, 128 * t:128 * t + 128]
                        if t == TILES - 1:
                            pe.matmul(SC[u % 2][:, 0:512], q, CK[F, :], start=True, stop=True)
                            mm = pe.matmul(SC[u % 2][:, 512:512 + NS], q, QK[F, 1, NP:NTOK], start=True, stop=True)
                        else:
                            c0, k = window(t)
                            if k > 1:
                                pe.matmul(SC[u % 2][:, c0:512], q, QK[F, 1, 128 * (t + 1 - k):128 * t], start=True, stop=True)
                            mm = pe.matmul(SC[u % 2][:, 512:640], q, QK[F, 1, 128 * t:128 * t + 128], start=True, stop=True)
                        mm.then_inc(s_done, 1)

                    def turn(u):
                        t = u // 2
                        pe.wait_ge(e_ok, n * UNITS + u + 1)
                        if u:
                            pe.wait_ge(et_a, n * UNITS + u)
                            pe.wait_ge(et_d, n * UNITS + u)
                        else:
                            pe.wait_ge(ko_ok, n + 1)
                        k = window(t)[1]
                        for m in range(5 - k, 5):
                            kw = NS if t == TILES - 1 and m == 4 else 128
                            mm = pe.transpose(PT[0:kw, 128 * m:128 * m + 128], E[:, u % 2, 128 * m:128 * m + kw], ident[:, :])
                        mm.then_inc(et_done, 1)

                    def values(u):
                        t, e = u // 2, u % 2
                        pe.wait_ge(et_a, n * UNITS + u + 1)
                        pe.wait_ge(et_d, n * UNITS + u + 1)
                        if u:
                            pe.wait_ge(o_ok, n * UNITS + u)
                        if t:
                            pe.wait_ge(of_ok, n * TILES + t)
                        k = window(t)[1]
                        for m in range(5 - k, 5):
                            if t == TILES - 1:
                                kw = NS if m == 4 else 128
                                v = VT[0:NS, 8, ds(n * 128 + 64 * e, 64)] if m == 4 else VC[:, m, ds(n * 128 + 64 * e, 64)]
                            else:
                                kw = 128
                                v = VT[:, t - 4 + m, ds(n * 128 + 64 * e, 64)]
                            mm = pe.matmul(PO[:, 64 * e:64 * e + 64], ET[0:kw, u % 2, 128 * m:128 * m + 128], v,
                                           start=m == 5 - k, stop=m == 4)
                        mm.then_inc(o_done, 1)

                    def turn_out(t):
                        pe.wait_ge(o_ok, n * UNITS + 2 * t + 2)
                        pe.transpose(PO[:, 256:384], OT[:, t % 2, :], ident[:, :]).then_inc(ot_done, 1)

                    for u in range(UNITS + 3):
                        if u < UNITS:
                            scores(u)
                        fill(PER_UNIT[0])
                        if 1 <= u <= UNITS:
                            turn(u - 1)
                        fill(PER_UNIT[1] + (u % 2) * PER_UNIT[2])
                        if u >= 3 and (u - 3) % 2:
                            turn_out((u - 3) // 2)
                        if 2 <= u <= UNITS + 1:
                            values(u - 2)
                    for _ in steps:
                        pass

                pair(0, True)
                with pe.Fori(1, PAIRS - 1) as n:
                    pair(n, True)
                pair(PAIRS - 1, False)

            @block.scalar
            def _(act):
                def pair(n, more):
                    left = list(range(9)) if more else []

                    def jobs(upto):
                        while left and left[0] <= upto:
                            proj_copy(act, n + 1, left.pop(0))

                    act.wait_ge(proj_out, n * 9 + 9)
                    for x in range(2):
                        wait(act, sums, n * 2)
                        act.activation(sq[:, x, 0:NTOK], raw[:, x, 0:NTOK], ACT.Square).then_inc(squared, 1)
                    wait(act, of_ok, n * TILES)
                    act.activation(zs[:, 0:NTOK], zraw[:, 0:NTOK], ACT.Silu).then_inc(z_ok, 1)
                    act.preload_act_table_set("natural_log_exp_and_others")
                    for x in range(2):
                        act.wait_ge(sums, n * 2 + x + 1)
                        wait(act, normed, n * 2)
                        act.activation(rs[:, x, 0:NP], SC[x][:, :], ACT.Ln, scale=1.0 / B_D, bias=eps[:, 0:1]).then_inc(lns, 1)
                        act.activation(rs[:, x, NP:NTOK], PT[:, 512 * x:512 * x + NS], ACT.Ln, scale=1.0 / B_D,
                                       bias=eps[:, 0:1]).then_inc(lns, 1)
                        act.wait_ge(lns, n * 4 + 2 * x + 2)
                        act.activation(rs[:, x, 0:NTOK], rs[:, x, 0:NTOK], ACT.Exp, scale=-0.5,
                                       bias=lnb[:, 0:1] if x == 0 else 0.0).then_inc(rs_ok, 1)
                        jobs(0)
                    for u in range(UNITS + 1):
                        if u < UNITS:
                            t = u // 2
                            c0 = window(t)[0]
                            c1 = 512 + NS if t == TILES - 1 else SPAN
                            act.wait_ge(ns_ok, n * UNITS + u + 1)
                            if u >= 2:
                                act.wait_ge(et_done, n * UNITS + u - 1)
                            else:
                                wait(act, et_done, n * UNITS)
                            wait(act, ri_ok, n * UNITS)
                            act.activation(E[:, u % 2, c0:c1], NS_[:, u % 2, c0:c1], ACT.Exp, scale=-1.0, bias=nm[:, u:u + 1],
                                           accum_out=rsum[:, u:u + 1]).then_inc(e_ok, 1)
                            jobs(steps_at(u) // 8 - 1)
                        if u:
                            v = u - 1
                            t = v // 2
                            c0, k = window(v // 2)
                            act.wait_ge(et_done, n * UNITS + v + 1)
                            if v >= 2:
                                act.wait_ge(o_done, n * UNITS + v - 1)
                            if k > 1:
                                src = PT[:, c0:512].rearrange("p (m q) -> p m q", q=128)
                                dst = ET[:, v % 2, c0:512].rearrange("p (m q) -> p m q", q=128)
                                act.activation(dst, src, ACT.Copy).then_inc(et_a, 1)
                            else:
                                act.activation(junk[:, 0:1], eps[:, 0:1], ACT.Copy).then_inc(et_a, 1)
                    jobs(8)
                    act.wait_ge(of_ok, n * TILES + TILES)
                    act.dma_start(o_dram[ds(n * 128 + 1024, 128), :], OF[:, 0:NTOK]).then_inc(st_o, 16)
                    act.wait_ge(ko_ok, n + 1)
                    act.dma_start(k_p[:, ds(n * 128, 128)].rearrange("(m p) d -> p m d", p=128), KO[:, 0:4, :]).then_inc(st_k, 16)
                    act.dma_start(k_s[:, ds(n * 128, 128)], KO[0:NS, 4, :]).then_inc(st_k, 16)

                pair(0, True)
                with act.Fori(1, PAIRS - 1) as n:
                    pair(n, True)
                pair(PAIRS - 1, False)
                act.wait_ge(st_o, PAIRS * 16)
                act.wait_ge(st_k, PAIRS * 32)

            @block.vector
            def _(dve):
                def pair(n):
                    for x in range(2):
                        dve.wait_ge(rs_ok, n * 2 + x + 1)
                        wait(dve, s_done, n * UNITS)
                        dve.scalar_tensor_tensor(QK[:, x, 0:NTOK], raw[:, x, 0:NTOK], g2[:, x:x + 1], rs[:, x, 0:NTOK],
                                                 ALU.mult, ALU.mult).then_inc(normed, 1)
                    dve.wait_ge(ck_done, n + 1)
                    dve.tensor_copy(CK[:, :], PO[:, :]).then_inc(ck_ok, 1)
                    dve.wait_ge(ko_done, n + 1)
                    wait(dve, st_k, n * 32)
                    dve.tensor_copy(KO[:, 0:4, :], PT[:, 0:512].rearrange("p (m d) -> p m d", m=4))
                    dve.tensor_copy(KO[0:NS, 4, :], PT[0:NS, 512:640]).then_inc(ko_ok, 1)
                    dve.wait_ge(bias_ok, n + 1)

                    def negate(u):
                        t, e = u // 2, u % 2
                        c0 = window(t)[0]
                        c1 = 512 + NS if t == TILES - 1 else SPAN
                        dve.wait_ge(s_done, n * UNITS + u + 1)
                        if u >= 2:
                            dve.wait_ge(e_ok, n * UNITS + u - 1)
                        else:
                            wait(dve, e_ok, n * UNITS)
                        dve.memset(tick[:, u:u + 1], 0.0)
                        dve.tensor_tensor_reduce(NS_[:, u % 2, c0:c1], SC[u % 2][:, c0:c1], bias[:, e, c0:c1], -1.0, 3e38,
                                                 ALU.add, ALU.min, nm[:, u:u + 1]).then_inc(ns_ok, 1)

                    def copy_turned(u):
                        t = u // 2
                        kw = NS if t == TILES - 1 else 128
                        dve.wait_ge(et_done, n * UNITS + u + 1)
                        if u >= 2:
                            dve.wait_ge(o_done, n * UNITS + u - 1)
                        dve.tensor_copy(ET[0:kw, u % 2, 512:640], PT[0:kw, 512:640]).then_inc(et_d, 1)

                    def normalise(u):
                        t, e = u // 2, u % 2
                        dve.reciprocal(rinv[:, u:u + 1], rsum[:, u:u + 1]).then_inc(ri_ok, 1)
                        dve.wait_ge(o_done, n * UNITS + u + 1)
                        dve.wait_ge(ri_ok, n * UNITS + u + 1)
                        if t >= 2:
                            dve.wait_ge(ot_done, n * TILES + t - 1)
                        dve.tensor_scalar(OT[:, t % 2, 64 * e:64 * e + 64], PO[:, 64 * e:64 * e + 64], rinv[:, u:u + 1],
                                          None, ALU.mult).then_inc(o_ok, 1)

                    def gate(t):
                        dve.wait_ge(ot_done, n * TILES + t + 1)
                        dve.wait_ge(z_ok, n + 1)
                        wait(dve, st_o, n * 16)
                        dve.tensor_tensor(OF[:, 128 * t:128 * t + 128], PO[:, 256:384], zs[:, 128 * t:128 * t + 128],
                                          ALU.mult).then_inc(of_ok, 1)

                    for u in range(UNITS + 3):
                        if u < UNITS:
                            negate(u)
                        if 1 <= u <= UNITS:
                            copy_turned(u - 1)
                        if u >= 3 and (u - 3) % 2:
                            gate((u - 3) // 2)
                        if 2 <= u <= UNITS + 1:
                            normalise(u - 2)

                pair(0)
                with dve.Fori(1, PAIRS - 1) as n:
                    pair(n)
                pair(PAIRS - 1)

            @block.gpsimd
            def _(pool):
                pool.memset(QK[:, :, NTOK:PAD], 0.0)
                pool.memset(unseen[:, :], 0.0).then_inc(mask0, 1)
                pool.wait_ge(mask0, 1)
                pool.memset(unseen[64:128, 0:CHUNK], NEG)
                pool.memset(unseen[0:64, SPAN - CHUNK:SPAN], NEG).then_inc(mask0, 1)
                pool.wait_ge(mask0, 2)
                pool.memset(zs[:, NTOK:PAD], 0.0)

                def pair(n):
                    pool.wait_ge(b_ld, n * 32 + 32)
                    wait(pool, ns_ok, n * UNITS)
                    pool.tensor_tensor(bias[:, :, :], stage[:, :, ::-1], unseen[:, :].unsqueeze(1).broadcast_to([128, 2, SPAN]),
                                       ALU.add).then_inc(bias_ok, 1)

                pair(0)
                with pool.Fori(1, PAIRS - 1) as n:
                    pair(n)
                pair(PAIRS - 1)


H_C, DV_C, RANK, TAU = 8, 256, 16, 16.0
MID = CHUNK // 2 - 1


GLA_SLOT = {"q": 0, "k": 1, "z0": 2, "z1": 3}
GLA_FIRST = {"q": 0, "k": 1024, "z0": 4112, "z1": 4112 + 128}


def gla_weights(W, w_ld, w_in):
    w_cols = w_in.rearrange("(k p) n -> p k n", p=128)
    return [(W[:, GLA_SLOT[x], :, :], w_cols[:, :, GLA_FIRST[x]:GLA_FIRST[x] + 128], w_ld[GLA_SLOT[x]])
            for x in ("z0", "z1", "q", "k")]


def gla(nc, ident, ones, eps, hT, W, w_ld, w_in, w_up, gate_bias, onorm_g, state_in, o_dram, state_p, state_s, ahead):
    w_cols = w_in.rearrange("(k p) n -> p k n", p=128)
    COL = {"q": 0, "k": 1024, "v": 2048, "lr": 4096, "z": 4112}
    with ExitStack() as ctx:
        def sb(n, shape):
            return ctx.enter_context(nc.sbuf_tensor("gla_" + n, shape, F32))

        sem = semaphores(nc, ctx, "gla_")

        lrT = sb("lrT", [RANK, NTOK])
        wup = sb("wup", [RANK, H_C * 128])
        gbias = sb("gbias", [128, H_C])
        onorm = sb("onorm", [128, 2])
        sall = sb("sall", [128, H_C, DV_C])
        seen = sb("seen", [128, 128])
        fresh = sb("fresh", [128, CW])

        with ExitStack() as sub:
            wlr = sub.enter_context(nc.sbuf_tensor("gla_wlr", [128, KD, RANK], F32))
            pl = sub.enter_context(nc.psum_tensor("gla_pl", [RANK, 3, 512], F32))
            ld, lr_done, masks, st = sem("ld"), sem("lr_done"), sem("masks"), sem("ld_st")
            with nc.Block() as block:
                @block.sync
                def _(sp):
                    sp.dma_start(wlr[:, :, :], w_cols[:, :, COL["lr"]:COL["lr"] + RANK]).then_inc(ld, 16)
                    sp.dma_start(wup[:, :], w_up).then_inc(st, 16)
                    sp.dma_start(gbias[:, :], gate_bias.rearrange("(h p) -> p h", p=128), allow_slow_non_contiguous=True).then_inc(st, 16)
                    sp.dma_start(onorm[:, :], onorm_g.rearrange("(h p) -> p h", p=128), allow_slow_non_contiguous=True).then_inc(st, 16)
                    sp.dma_start(sall[:, :, :], state_in.rearrange("h d v -> d h v")).then_inc(st, 16)
                    sp.wait_ge(st, 64)

                @block.tensor
                def _(pe):
                    pe.wait_ge(ld, 16)
                    for c, (c0, w) in enumerate(BANKS):
                        for k in range(KD):
                            mm = pe.matmul(pl[:, c, 0:w], wlr[:, k, :], hT[:, k, c0:c0 + w], start=k == 0, stop=k == KD - 1)
                    mm.then_inc(lr_done, 1)

                @block.vector
                def _(dve):
                    dve.wait_ge(lr_done, 1)
                    dve.tensor_copy(lrT[:, :], pl[:, :, :].rearrange("p c n -> p (c n)")[:, 0:NTOK])

                @block.gpsimd
                def _(pool):
                    pool.memset(fresh[:, :], 1.0).then_inc(masks, 1)
                    pool.memset(seen[:, :], 1.0).then_inc(masks, 1)
                    pool.wait_ge(masks, 2)
                    pool.memset(fresh[:, :].rearrange("p (c n) -> p c n", n=CHUNK)[:, :, 0:1], 0.0)
                    pool.affine_select(out=seen[:, :], in_=seen[:, :], compare_op=ALU.is_ge, fill=0.0, base=0,
                                       pattern=[[1, 128]], channel_multiplier=-1).then_inc(masks, 1)
                    pool.wait_ge(masks, 3)
                    pool.memset(seen[0:CHUNK, CHUNK:128], 0.0)

        Wv = sb("Wv", [128, KD, DV_C])
        raw = sb("raw", [128, 2, NTOK])
        zraw = sb("zraw", [128, 2, NTOK])
        zs = sb("zs", [128, 2, NTOK])
        vraw = sb("vraw", [128, TILES, DV_C])
        V = sb("V", [128, TILES, DV_C])
        tmp = sb("tmp", [128, 2, CW])
        CB = sb("CB", [128, CW])
        lg = sb("lg", [128, CW])
        E1 = sb("E1", [128, CW])
        E2 = sb("E2", [128, CW])
        em = sb("em", [128, NCH + 1])
        el = sb("el", [128, NCH + 1])
        QG = sb("QG", [128, PAD])
        KG = sb("KG", [128, PAD])
        AT = sb("AT", [128, TILES, 128])
        KT = sb("KT", [128, TILES, 128])
        PS = sb("PS", [128, 2, DV_C])
        S = sb("S", [128, 2, DV_C])
        SM = sb("SM", [128, 2, DV_C])
        Ss = sb("Ss", [128, DV_C])
        Sn = sb("Sn", [128, DV_C])
        OF = sb("OF", [128, 2, CW])
        rs = sb("rs", [128, CW])
        wgc = sb("wgc", [RANK, 128])
        gbc = sb("gbc", [128, 1])
        zeros = sb("zeros", [128, 1])
        pj = ctx.enter_context(nc.psum_tensor("gla_pj", [128, 2, 512], F32))
        X = ctx.enter_context(nc.psum_tensor("gla_X", [128, 3, 512], F32))
        PP = ctx.enter_context(nc.psum_tensor("gla_PP", [128, 512], F32))
        O = ctx.enter_context(nc.psum_tensor("gla_O", [128, 2, 512], F32))
        Xf = X[:, :, :].rearrange("p b n -> p (b n)")
        PB = [X[:, 2, 0:DV_C], PP[:, 0:DV_C]]

        wv_ld = sem("wv_ld")
        proj_done, proj_out, padded, picked, z_ok, v_ok = (sem("proj_done"), sem("proj_out"), sem("padded"), sem("picked"),
                                                          sem("z_ok"), sem("v_ok"))
        g_done, y_ok, sp_ok, lg_ok, cb_ok, d_ok, e_ok, q_ok = (sem("g_done"), sem("y_ok"), sem("sp_ok"), sem("lg_ok"), sem("cb_ok"),
                                                              sem("d_ok"), sem("e_ok"), sem("q_ok"))
        at_done, at_ok, kt_done, kt_ok = sem("at_done"), sem("at_ok"), sem("kt_done"), sem("kt_ok")
        ss_ok, s_zero, p_done, ps_ok, s_ok, sm_ok, o_done, o_out = (sem("ss_ok"), sem("s_zero"), sem("p_done"), sem("ps_ok"), sem("s_ok"),
                                                                   sem("sm_ok"), sem("o_done"), sem("o_out"))
        o_sq, o_sum, o_rs, o_fin, st_p, st_s, st_o = (sem("o_sq"), sem("o_sum"), sem("o_rs"), sem("o_fin"), sem("st_p"), sem("st_s"),
                                                     sem("st_o"))

        PLAN = ([("z0", c) for c in JOBS] + [("z1", c) for c in JOBS] + [("v", t) for t in range(TILES)]
                + [("q", c) for c in JOBS] + [("k", c) for c in JOBS])
        NJ = len(PLAN)
        SLOT, FIRST = GLA_SLOT, GLA_FIRST
        STRIDE = {"q": 128, "k": 128, "z0": 256, "z1": 256}
        LAST = {kind: max(m for m, (x, _) in enumerate(PLAN) if x == kind) for kind in ("z0", "z1", "v", "q", "k")}
        LEAD, START, PER_GROUP, PER_CHUNK = 8, 38, 7, 6

        def chunk(c):
            t, a = c // 2, c % 2
            return t, a, slice(64 * a, 64 * a + 64)

        def by_chunk(buf):
            return buf[:, :].rearrange("p (c n) -> p c n", n=CHUNK)

        with nc.Block() as block:
            @block.sync
            def _(sp):
                def load(n, kind):
                    if kind == "v":
                        sp.dma_start(Wv[:, :, :], w_cols[:, :, ds(n * DV_C + COL["v"], DV_C)]).then_inc(wv_ld, 16)
                    else:
                        sp.dma_start(W[:, SLOT[kind], :, :], w_cols[:, :, ds(n * STRIDE[kind] + FIRST[kind], 128)]).then_inc(w_ld[SLOT[kind]], 16)

                load(0, "v")
                with sp.Fori(0, H_C - 1) as h:
                    for kind, m in LAST.items():
                        sp.wait_ge(proj_done, h * NJ + m + 1)
                        load(h + 1, kind)
                sp.wait_ge(proj_done, H_C * NJ)
                load_ahead(sp, ahead)

            @block.tensor
            def _(pe):
                def project(n):
                    for m, (kind, x) in enumerate(PLAN):
                        if kind == "v":
                            wait(pe, wv_ld, n * 16 + 16)
                        else:
                            wait(pe, w_ld[SLOT[kind]], n * 16 + 16)
                        wait(pe, proj_out, n * NJ + max(m - 1, 0))
                        for k in range(KD):
                            if kind == "v":
                                mm = pe.matmul(pj[:, m % 2, 0:DV_C], hT[:, k, 128 * x:128 * x + 128], Wv[:, k, :],
                                               start=k == 0, stop=k == KD - 1)
                            else:
                                c0, w = x
                                mm = pe.matmul(pj[:, m % 2, 0:w], W[:, SLOT[kind], k, :], hT[:, k, c0:c0 + w],
                                               start=k == 0, stop=k == KD - 1)
                            if k == KD - 1:
                                mm.then_inc(proj_done, 1)
                            yield

                def head(h, more):
                    steps = project(h + 1) if more else iter(())

                    def fill(k):
                        for _ in range(k):
                            next(steps, None)

                    fill(LEAD)
                    pe.wait_ge(picked, h * 2 + 2)
                    wait(pe, o_rs, h * 2)
                    for c, (c0, w) in enumerate(BANKS):
                        mm = pe.matmul(X[:, c, 0:w], wgc[:, :], lrT[:, c0:c0 + w], start=True, stop=True)
                    mm.then_inc(g_done, 1)
                    fill(START - LEAD)
                    pe.wait_ge(q_ok, h * 2 + 2)
                    for g in range(3):
                        if g:
                            pe.wait_ge(at_ok, h * 3 + g)
                        for t in range(3 * g, 3 * g + 3):
                            c = 128 * (t - 3 * g)
                            mm = pe.matmul(X[:, 0, c:c + 128], KG[:, 128 * t:128 * t + 128], QG[:, 128 * t:128 * t + 128],
                                           start=True, stop=True)
                        mm.then_inc(at_done, 1)
                        if g:
                            pe.wait_ge(kt_ok, h * 3 + g)
                        for t in range(3 * g, 3 * g + 3):
                            c = 128 * (t - 3 * g)
                            mm = pe.transpose(X[:, 1, c:c + 128], KG[:, 128 * t:128 * t + 128], ident[:, :])
                        mm.then_inc(kt_done, 1)
                        fill(PER_GROUP)
                    pe.wait_ge(v_ok, h + 1)
                    for c in range(NCH + 1):
                        t, a, P = chunk(c)
                        if c == 0:
                            pe.wait_ge(kt_ok, h * 3 + 3)
                            pe.wait_ge(at_ok, h * 3 + 3)
                        if c >= 2:
                            pe.wait_ge(ps_ok, h * 17 + c - 1)
                        pe.matmul(PB[c % 2], KT[P, t, :], V[P, t, :], start=True, stop=True).then_inc(p_done, 1)
                        fill(PER_CHUNK)
                        if c in (0, 8, 16):
                            wait(pe, o_out, h * 3 + c // 8)
                        pe.wait_ge(sm_ok, h * 17 + c + 1)
                        for v in range(2):
                            o = O[:, v, 64 * (c % 8):64 * (c % 8) + 64]
                            pe.matmul(o, SM[:, c % 2, 128 * v:128 * v + 128], QG[:, 64 * c:64 * c + 64], start=True, stop=False)
                            mm = pe.matmul(o, V[:, t, 128 * v:128 * v + 128], AT[:, t, 64 * a:64 * a + 64], start=False, stop=True)
                        mm.then_inc(o_done, 1)
                    for _ in steps:
                        pass
                    pe.wait_ge(o_sq, h + 1)
                    pe.wait_ge(ps_ok, h * 17 + 17)
                    for b, w in ((0, 512), (1, 512), (2, CW - 1024)):
                        for v in range(2):
                            mm = pe.matmul(X[:, b, 0:w], ones[:, :], tmp[:, v, 512 * b:512 * b + w], start=v == 0, stop=v == 1)
                    mm.then_inc(o_sum, 1)

                for _ in project(0):
                    pass
                head(0, True)
                with pe.Fori(1, H_C - 1) as h:
                    head(h, True)
                head(H_C - 1, False)

            @block.scalar
            def _(act):
                def proj_copy(n, m):
                    kind, x = PLAN[m]
                    act.wait_ge(proj_done, n * NJ + m + 1)
                    if kind == "v":
                        wait(act, v_ok, n * 1)
                        act.activation(vraw[:, x, :], pj[:, m % 2, 0:DV_C], ACT.Copy).then_inc(proj_out, 1)
                        return
                    c0, w = x
                    if kind[0] == "z":
                        wait(act, z_ok, n * 1)
                        dst = zraw[:, int(kind[1]), c0:c0 + w]
                    else:
                        wait(act, q_ok, n * 2)
                        dst = raw[:, SLOT[kind], c0:c0 + w]
                    act.activation(dst, pj[:, m % 2, 0:w], ACT.Copy, scale=128.0 ** -0.5 if kind == "q" else 1.0).then_inc(proj_out, 1)

                def head(h, more):
                    left = list(range(NJ)) if more else []

                    def jobs(steps):
                        while left and 8 * (left[0] + 1) <= steps:
                            proj_copy(h + 1, left.pop(0))

                    act.wait_ge(proj_out, h * NJ + NJ)
                    wait(act, o_fin, h * 3)
                    act.activation(zs[:, :, :], zraw[:, :, :], ACT.Silu).then_inc(z_ok, 1)
                    act.preload_act_table_set("natural_log_exp_and_others")
                    act.wait_ge(g_done, h + 1)
                    act.wait_ge(picked, h * 2 + 2)
                    act.activation(tmp[:, 0, 0:NTOK], Xf[:, 0:NTOK], ACT.Identity, bias=gbc[:, 0:1]).then_inc(y_ok, 1)
                    jobs(8)
                    act.wait_ge(y_ok, h + 1)
                    act.activation(tmp[:, 1, 0:NTOK], tmp[:, 0, 0:NTOK], ACT.Abs).then_inc(sp_ok, 1)
                    act.wait_ge(sp_ok, h * 3 + 1)
                    act.activation(tmp[:, 1, 0:NTOK], tmp[:, 1, 0:NTOK], ACT.Exp, scale=-1.0).then_inc(sp_ok, 1)
                    act.wait_ge(sp_ok, h * 3 + 2)
                    act.activation(tmp[:, 1, 0:NTOK], tmp[:, 1, 0:NTOK], ACT.Ln, bias=1.0).then_inc(sp_ok, 1)
                    jobs(START)
                    act.wait_ge(cb_ok, h + 1)
                    wait(act, sm_ok, h * 17)
                    wait(act, s_ok, h * 17)
                    act.activation(em[:, :].unsqueeze(2), by_chunk(CB)[:, :, MID:MID + 1], ACT.Exp, scale=1.0 / TAU).then_inc(e_ok, 1)
                    act.activation(el[:, :].unsqueeze(2), by_chunk(CB)[:, :, CHUNK - 1:CHUNK], ACT.Exp, scale=1.0 / TAU).then_inc(e_ok, 1)
                    act.wait_ge(d_ok, h + 1)
                    wait(act, q_ok, h * 2)
                    act.activation(E1[:, :], lg[:, :], ACT.Exp, scale=1.0 / TAU).then_inc(e_ok, 1)
                    act.activation(E2[:, :], lg[:, :], ACT.Exp, scale=-1.0 / TAU).then_inc(e_ok, 1)
                    for g in range(3):
                        act.wait_ge(kt_done, h * 3 + g + 1)
                        wait(act, p_done, h * 17)
                        act.activation(KT[:, 3 * g:3 * g + 3, :], X[:, 1, 0:384].rearrange("p (t n) -> p t n", t=3), ACT.Copy).then_inc(kt_ok, 1)
                        jobs(START + PER_GROUP * g)
                    for c in range(NCH + 1):
                        act.wait_ge(p_done, h * 17 + c + 1)
                        if c >= 2:
                            act.wait_ge(s_ok, h * 17 + c - 1)
                        else:
                            wait(act, s_ok, h * 17)
                        act.wait_ge(e_ok, h * 4 + 4)
                        act.activation(PS[:, c % 2, :], PB[c % 2], ACT.Copy, scale=E1[:, 64 * c + 63:64 * c + 64]).then_inc(ps_ok, 1)
                        jobs(START + 3 * PER_GROUP + PER_CHUNK * c)
                        if c in (8, 16):
                            b = c // 8 - 1
                            act.wait_ge(o_done, h * 17 + c)
                            if b == 0:
                                wait(act, st_o, h * 32)
                            act.activation(OF[:, :, 512 * b:512 * b + 512], O[:, :, :], ACT.Copy).then_inc(o_out, 1)
                    act.wait_ge(o_done, h * 17 + 17)
                    act.activation(OF[:, :, 1024:CW], O[:, :, 0:64], ACT.Copy).then_inc(o_out, 1)
                    act.wait_ge(o_out, h * 3 + 3)
                    act.wait_ge(lg_ok, h + 1)
                    act.activation(tmp[:, :, :], OF[:, :, :], ACT.Square).then_inc(o_sq, 1)
                    jobs(8 * NJ)
                    act.wait_ge(o_sum, h + 1)
                    act.activation(rs[:, :], Xf[:, 0:CW], ACT.Ln, scale=1.0 / DV_C, bias=eps[:, 0:1]).then_inc(o_rs, 1)
                    act.wait_ge(o_rs, h * 2 + 1)
                    act.activation(rs[:, :], rs[:, :], ACT.Exp, scale=-0.5).then_inc(o_rs, 1)
                    act.wait_ge(s_ok, h * 17 + 17)
                    act.dma_start(state_p[ds(h, 1), :, :].rearrange("o d v -> d (o v)"), S[:, 0, :]).then_inc(st_p, 16)
                    act.dma_start(state_s[ds(h, 1), :, :].rearrange("o d v -> d (o v)"), Sn[:, :]).then_inc(st_s, 16)
                    act.wait_ge(o_fin, h * 3 + 3)
                    for v in range(2):
                        act.dma_start(o_dram[ds(h * DV_C + 128 * v, 128), :], OF[:, v, 0:NTOK]).then_inc(st_o, 16)

                for m in range(NJ):
                    proj_copy(0, m)
                head(0, True)
                with act.Fori(1, H_C - 1) as h:
                    head(h, True)
                head(H_C - 1, False)
                act.wait_ge(st_p, H_C * 16)
                act.wait_ge(st_s, H_C * 16)
                act.wait_ge(st_o, H_C * 32)

            @block.vector
            def _(dve):
                dve.memset(lg[:, NTOK:CW], 0.0)
                dve.memset(zeros[:, :], 0.0).then_inc(padded, 1)

                def head(h):
                    wait(dve, st_p, h * 16)
                    wait(dve, o_done, h * 17)
                    dve.memset(S[:, 0, :], 0.0).then_inc(s_zero, 1)
                    dve.wait_ge(proj_out, h * NJ + NJ)
                    dve.tensor_copy(V[:, :, :], vraw[:, :, :]).then_inc(v_ok, 1)
                    dve.wait_ge(sp_ok, h * 3 + 3)
                    wait(dve, e_ok, h * 4)
                    dve.scalar_tensor_tensor(lg[:, 0:NTOK], tmp[:, 0, 0:NTOK], 0.0, tmp[:, 1, 0:NTOK], ALU.min, ALU.subtract).then_inc(lg_ok, 1)
                    dve.wait_ge(lg_ok, h + 1)
                    dve.memset(lg[:, NTOK:CW], 0.0).then_inc(padded, 1)
                    dve.wait_ge(padded, h + 2)
                    dve.tensor_tensor_scan(CB[:, :], fresh[:, :], lg[:, :], 0.0, ALU.mult, ALU.add).then_inc(cb_ok, 1)
                    dve.wait_ge(cb_ok, h + 1)
                    dve.tensor_tensor(by_chunk(lg), by_chunk(CB), by_chunk(CB)[:, :, MID:MID + 1].broadcast_to([128, NCH + 1, CHUNK]),
                                      ALU.subtract).then_inc(d_ok, 1)
                    for x, (dst, e) in enumerate(((QG, E1), (KG, E2))):
                        dve.wait_ge(e_ok, h * 4 + 3 + x)
                        if x == 0:
                            wait(dve, o_done, h * 17)
                        else:
                            wait(dve, kt_done, h * 3)
                        dve.tensor_tensor(dst[:, 0:NTOK], raw[:, x, :], e[:, 0:NTOK], ALU.mult).then_inc(q_ok, 1)
                    for g in range(3):
                        dve.wait_ge(at_done, h * 3 + g + 1)
                        dve.tensor_tensor(AT[:, 3 * g:3 * g + 3, :], X[:, 0, 0:384].rearrange("p (t n) -> p t n", t=3),
                                          seen[:, :].unsqueeze(1).broadcast_to([128, 3, 128]), ALU.mult).then_inc(at_ok, 1)
                    for c in range(NCH + 1):
                        src = S[:, c % 2, :] if c < NCH else Ss[:, :]
                        dst = S[:, (c + 1) % 2, :] if c < NCH else Sn[:, :]
                        if c == 0:
                            dve.wait_ge(s_zero, h + 1)
                        elif c < NCH:
                            dve.wait_ge(s_ok, h * 17 + c)
                        else:
                            dve.wait_ge(ss_ok, h + 1)
                            wait(dve, st_s, h * 16)
                        if c >= 2:
                            dve.wait_ge(o_done, h * 17 + c - 1)
                        dve.tensor_scalar(SM[:, c % 2, :], src, em[:, c:c + 1], None, ALU.mult).then_inc(sm_ok, 1)
                        dve.wait_ge(ps_ok, h * 17 + c + 1)
                        if c:
                            dve.wait_ge(sm_ok, h * 17 + c)
                        dve.scalar_tensor_tensor(dst, src, el[:, c:c + 1], PS[:, c % 2, :], ALU.mult, ALU.add).then_inc(s_ok, 1)
                    dve.wait_ge(o_rs, h * 2 + 2)
                    dve.tensor_tensor(OF[:, :, :], OF[:, :, :], rs[:, :].unsqueeze(1).broadcast_to([128, 2, CW]), ALU.mult).then_inc(o_fin, 1)
                    dve.wait_ge(o_fin, h * 3 + 1)
                    dve.wait_ge(z_ok, h + 1)
                    for v in range(2):
                        dve.scalar_tensor_tensor(OF[:, v, 0:NTOK], OF[:, v, 0:NTOK], onorm[:, v:v + 1], zs[:, v, :],
                                                 ALU.mult, ALU.mult).then_inc(o_fin, 1)

                head(0)
                with dve.Fori(1, H_C - 1) as h:
                    head(h)
                head(H_C - 1)

            @block.gpsimd
            def _(pool):
                pool.memset(QG[:, NTOK:PAD], 0.0)
                pool.memset(KG[:, NTOK:PAD], 0.0)

                def head(h):
                    wait(pool, g_done, h * 1)
                    wait(pool, y_ok, h * 1)
                    pool.tensor_copy(wgc[:, :], wup[:, ds(h * 128, 128)]).then_inc(picked, 1)
                    pool.tensor_copy(gbc[:, :], gbias[:, ds(h, 1)]).then_inc(picked, 1)
                    wait(pool, s_ok, h * 17)
                    wait(pool, sm_ok, h * 17)
                    pool.tensor_copy(Ss[:, :], sall[:, ds(h, 1), :].rearrange("p o n -> p (o n)")).then_inc(ss_ok, 1)

                head(0)
                with pool.Fori(1, H_C - 1) as h:
                    head(h)
                head(H_C - 1)


def flat(ap):
    return ap.rearrange("b l h d -> (b l) (h d)")


def finish_layer(nc, l, ident, ones, eps, hT, part0, w_out, w_mq, w_mo, mnorm_g, mq_g, o_dram, om_dram,
                 x_in, x_mid, x_out, next_gain, kv_prompt, kv_sample, ahead):
    with ExitStack() as ctx:
        sem = semaphores(nc, ctx, f"finish{l}_")
        Wq = ctx.enter_context(nc.sbuf_tensor(f"finish{l}_Wq", [128, KD, 2 * M_H * M_D], F32))
        Wo = ctx.enter_context(nc.sbuf_tensor(f"finish{l}_Wo", [128, M_H, D], F32))
        q_ld, o_ld = [sem(f"q_ld{q}") for q in range(4)], [sem(f"o_ld{q}") for q in range(PARTS)]
        parts = [(Wo[:, q:q + 1, :], o_ld[q]) for q in range(PARTS)]
        project_out(nc, f"out{l}", ident, eps, 16, w_out, [part0], o_dram, x_in, x_mid, mnorm_g, hT,
                    query_weights(Wq, q_ld, w_mq) + [out_weights(*part, w_mo, M_H, q) for q, part in enumerate(parts)])
        memory_attend(nc, f"mem{l}", ident, ones, eps, hT, Wq, q_ld, mq_g, kv_prompt, kv_sample, om_dram)
        project_out(nc, f"mo{l}", ident, eps, M_H, w_mo, parts, om_dram, x_mid, x_out, next_gain, hT, ahead)


def hybrid_streaming_encoder_step(nc, x_prompt, x_sample, mem_prompt, state_l0_gdn_conv, state_l0_gdn,
        cache_l0_band_k, cache_l0_band_v, cache_l0_mem_k, cache_l0_mem_v, state_l1_gla, cache_l1_mem_k,
        cache_l1_mem_v, l0_norm_g, l0_w_in, l0_conv_w, l0_a_log, l0_dt_bias, l0_a_onorm_g, l0_b_q_g, l0_b_k_g,
        l0_b_rel_bias, l0_w_out, l0_mnorm_g, l0_mem_norm_g, l0_w_mkv, l0_mk_g, l0_w_mq, l0_mq_g, l0_w_mo, l1_norm_g,
        l1_w_in, l1_w_gate_up, l1_gate_bias, l1_c_onorm_g, l1_w_out, l1_mnorm_g, l1_mem_norm_g, l1_w_mkv, l1_mk_g,
        l1_w_mq, l1_mq_g, l1_w_mo, outputs):
    (y_prompt, y_sample, p_gdn_conv, p_gdn, p_band_k, p_band_v, p_mem0_k, p_mem0_v, p_gla, p_mem1_k, p_mem1_v,
     s_gdn_conv, s_gdn, s_band_k, s_band_v, s_gla) = outputs
    group = "b l d -> (b l) d"
    state = "b h k v -> (b h) k v"

    def scratch(name, shape):
        return nc.dram_tensor(name, shape, F32).ap()

    o_dram = scratch("o_features", [2048, NTOK])
    om_dram = scratch("om_features", [512, NTOK])
    gate_rows = scratch("gate_rows", [2, H_A, PAD])
    bias_rows = scratch("bias_rows", [B_H, 768])
    x = [(scratch(f"x{i}_prompt", [NP, D]), scratch(f"x{i}_sample", [NS, D])) for i in range(3)]
    x_in = (x_prompt.rearrange(group), x_sample.rearrange(group))
    y = (y_prompt.rearrange(group), y_sample.rearrange(group))

    with ExitStack() as ctx:
        ident = identity(nc, ctx)
        hT = ctx.enter_context(nc.sbuf_tensor("hT", [128, KD, PAD], F32))
        ones = ctx.enter_context(nc.sbuf_tensor("ones", [128, 128], F32))
        eps = ctx.enter_context(nc.sbuf_tensor("eps", [128, 1], F32))
        with nc.Block() as block:
            @block.vector
            def _(dve):
                dve.memset(hT[:, :, NTOK:PAD], 0.0)
                dve.memset(ones[:, :], 1.0)
                dve.memset(eps[:, :], EPS)

        sem = semaphores(nc, ctx, "w_")
        Wb = ctx.enter_context(nc.sbuf_tensor("Wb", [128, 4 * KD * 128], F32))
        W_head = Wb[:, :].rearrange("p (j k n) -> p j k n", j=4, k=KD)
        W_part = Wb[:, :].rearrange("p (k n) -> p k n", n=D)
        gdn_ld, band_ld, gla_ld = ([sem(f"{x}{j}") for j in range(4)] for x in ("gdn", "band", "gla"))
        out_ld = [sem("out0"), sem("out1")]

        mem_kv = [(flat(p_mem0_k), flat(p_mem0_v)), (flat(p_mem1_k), flat(p_mem1_v))]
        memory_kv(nc, ident, eps, mem_prompt.rearrange(group),
                  [(l0_mem_norm_g, l0_w_mkv, l0_mk_g, *mem_kv[0]), (l1_mem_norm_g, l1_w_mkv, l1_mk_g, *mem_kv[1])],
                  gdn_weights(W_head, gdn_ld, l0_w_in))

        project_out(nc, "norm0", ident, eps, 0, None, (), None, x_in, None, l0_norm_g, hT)
        gdn(nc, ident, ones, eps, hT, W_head, gdn_ld, l0_w_in, l0_conv_w, state_l0_gdn_conv.rearrange(group), l0_a_log, l0_dt_bias,
            l0_a_onorm_g, state_l0_gdn.rearrange(state), gate_rows, o_dram, p_gdn_conv.rearrange(group),
            s_gdn_conv.rearrange(group), p_gdn.rearrange(state), s_gdn.rearrange(state),
            band_weights(W_head, band_ld, l0_w_in))
        band(nc, ident, ones, eps, hT, W_head, band_ld, l0_w_in, l0_b_q_g, l0_b_k_g, l0_b_rel_bias, flat(cache_l0_band_k),
             flat(cache_l0_band_v), bias_rows, o_dram, flat(p_band_k), flat(p_band_v), flat(s_band_k), flat(s_band_v),
             [out_weights(W_part, out_ld[0], l0_w_out, 16, 0)])
        finish_layer(nc, 0, ident, ones, eps, hT, (W_part, out_ld[0]), l0_w_out, l0_w_mq, l0_w_mo, l0_mnorm_g, l0_mq_g,
                     o_dram, om_dram, x_in, x[0], x[1], l1_norm_g, mem_kv[0],
                     (flat(cache_l0_mem_k), flat(cache_l0_mem_v)), gla_weights(W_head, gla_ld, l1_w_in))

        gla(nc, ident, ones, eps, hT, W_head, gla_ld, l1_w_in, l1_w_gate_up, l1_gate_bias, l1_c_onorm_g, state_l1_gla.rearrange(state),
            o_dram, p_gla.rearrange(state), s_gla.rearrange(state),
            [out_weights(W_part, out_ld[1], l1_w_out, 16, 0)])
        finish_layer(nc, 1, ident, ones, eps, hT, (W_part, out_ld[1]), l1_w_out, l1_w_mq, l1_w_mo, l1_mnorm_g, l1_mq_g,
                     o_dram, om_dram, x[1], x[2], y, None, mem_kv[1],
                     (flat(cache_l1_mem_k), flat(cache_l1_mem_v)), ())


_INS = ['x_prompt', 'x_sample', 'mem_prompt', 'state_l0_gdn_conv', 'state_l0_gdn', 'cache_l0_band_k',
        'cache_l0_band_v', 'cache_l0_mem_k', 'cache_l0_mem_v', 'state_l1_gla', 'cache_l1_mem_k', 'cache_l1_mem_v',
        'l0_norm_g', 'l0_w_in', 'l0_conv_w', 'l0_a_log', 'l0_dt_bias', 'l0_a_onorm_g', 'l0_b_q_g', 'l0_b_k_g',
        'l0_b_rel_bias', 'l0_w_out', 'l0_mnorm_g', 'l0_mem_norm_g', 'l0_w_mkv', 'l0_mk_g', 'l0_w_mq', 'l0_mq_g',
        'l0_w_mo', 'l1_norm_g', 'l1_w_in', 'l1_w_gate_up', 'l1_gate_bias', 'l1_c_onorm_g', 'l1_w_out', 'l1_mnorm_g',
        'l1_mem_norm_g', 'l1_w_mkv', 'l1_mk_g', 'l1_w_mq', 'l1_mq_g', 'l1_w_mo']
_OUTS = [(1, 1024, 1024), (1, 32, 1024), (1, 3, 3072), (1, 8, 128, 128), (1, 512, 16, 64), (1, 512, 16, 64),
         (1, 256, 4, 128), (1, 256, 4, 128), (1, 8, 128, 256), (1, 256, 4, 128), (1, 256, 4, 128),
         (1, 3, 3072), (1, 8, 128, 128), (1, 32, 16, 64), (1, 32, 16, 64), (1, 8, 128, 256)]


def kernel(**inputs):
    import numpy as _np
    import concourse.bacc as _bacc
    from concourse import mybir as _mybir
    from concourse.bass_utils import run_bass_kernel_spmd as _run

    nc = _bacc.Bacc("TRN2", target_bir_lowering=False, num_devices=1)
    arrays, args = {}, []
    for name in _INS:
        a = _np.ascontiguousarray(inputs[name])
        arrays[f"in_{name}_dram"] = a
        args.append(nc.dram_tensor(f"in_{name}_dram", a.shape, _mybir.dt.from_np(a.dtype), kind="ExternalInput").ap())
    outs = [nc.dram_tensor(f"out_{i}_dram", shape, _mybir.dt.from_np(_np.dtype("float32")), kind="ExternalOutput").ap()
            for i, shape in enumerate(_OUTS)]
    hybrid_streaming_encoder_step(nc, *args, outs)
    r = _run(nc, [arrays], core_ids=[0])
    return tuple(r.results[0][f"out_{i}_dram"] for i in range(len(_OUTS)))
```
